# Optimizing a Trainium2 kernel written in Bass

```python
import math
import jax, jax.numpy as jnp
from jax import lax
import numpy as np

D_MODEL = 1024
BATCH = 1
SEQ = 1024
DEPTH = 1

N_HEADS = 16
N_KV_HEADS = 2
HEAD_DIM = 64
GROUP = N_HEADS // N_KV_HEADS
ATTN_WIDTH = N_HEADS * HEAD_DIM
KV_WIDTH = N_KV_HEADS * HEAD_DIM
WINDOW = 128
BLOCK = 128
NUM_BUCKETS = 32
MAX_DISTANCE = 128
CONV_WIDTH = D_MODEL
CONV_KERNEL = 31
MEM_LEN = 256
MEM_HEADS = 4
MEM_HEAD_DIM = 256
MEM_WIDTH = MEM_HEADS * MEM_HEAD_DIM
N_BRANCHES = 3
SPLIT_SIZES = (ATTN_WIDTH, KV_WIDTH, KV_WIDTH, ATTN_WIDTH,
               2 * CONV_WIDTH, CONV_WIDTH,
               MEM_WIDTH, MEM_WIDTH,
               N_BRANCHES * D_MODEL)
IN_WIDTH = sum(SPLIT_SIZES)
SPLIT_POINTS = tuple(int(v) for v in np.cumsum(SPLIT_SIZES)[:-1])
RMS_EPS = 1e-6
LN_EPS = 1e-5

kernel_name = "hybrid_swa_conformer_memxattn_gated_block"

def rms_norm(x, g):
    xf = x.astype(jnp.float32)
    y = xf * lax.rsqrt(jnp.mean(xf * xf, axis=-1, keepdims=True) + RMS_EPS)
    return (y * g.astype(jnp.float32)).astype(x.dtype)

def layer_norm(x, g, b):
    xf = x.astype(jnp.float32)
    mu = jnp.mean(xf, axis=-1, keepdims=True)
    var = jnp.mean(jnp.square(xf - mu), axis=-1, keepdims=True)
    y = (xf - mu) * lax.rsqrt(var + LN_EPS)
    return (y * g.astype(jnp.float32) + b.astype(jnp.float32)).astype(x.dtype)

def t5_bucket(rel):
    n = jnp.maximum(rel, 0)
    max_exact = NUM_BUCKETS // 2
    nf = jnp.maximum(n, 1).astype(jnp.float32)
    large = max_exact + (jnp.log(nf / max_exact) / math.log(MAX_DISTANCE / max_exact)
                         * (NUM_BUCKETS - max_exact)).astype(jnp.int32)
    large = jnp.minimum(large, NUM_BUCKETS - 1)
    return jnp.where(n < max_exact, n, large)

def sliding_window_attention(q, k, v, sinks, rel_bias):
    B, S = q.shape[0], q.shape[1]
    nb = S // BLOCK
    qb = q.reshape(B, nb, BLOCK, N_KV_HEADS, GROUP, HEAD_DIM).astype(jnp.float32)

    def band(t):
        tb = t.reshape(B, nb, BLOCK, N_KV_HEADS, HEAD_DIM)
        prev = jnp.pad(tb, ((0, 0), (1, 0), (0, 0), (0, 0), (0, 0)))[:, :-1]
        return jnp.concatenate([prev, tb], axis=2)

    kb, vb = band(k), band(v)
    s = jnp.einsum('bnqkgd,bnjkd->bnkgqj', qb, kb.astype(jnp.float32)) * (HEAD_DIM ** -0.5)

    qi = jnp.arange(BLOCK)[:, None] + BLOCK
    kj = jnp.arange(2 * BLOCK)[None, :]
    rel = qi - kj
    bias = rel_bias.astype(jnp.float32)[t5_bucket(rel)]
    bias = bias.reshape(BLOCK, 2 * BLOCK, N_KV_HEADS, GROUP).transpose(2, 3, 0, 1)
    s = s + bias

    key_abs = jnp.arange(nb)[:, None, None] * BLOCK - BLOCK + kj[None]
    mask = ((rel >= 0) & (rel < WINDOW))[None] & (key_abs >= 0)
    s = jnp.where(mask[None, :, None, None], s, -1e30)

    sink = jnp.broadcast_to(sinks.astype(jnp.float32).reshape(N_KV_HEADS, GROUP)[None, None, :, :, None, None],
                            s.shape[:-1] + (1,))
    p = jax.nn.softmax(jnp.concatenate([s, sink], axis=-1), axis=-1)[..., :-1]
    o = jnp.einsum('bnkgqj,bnjkd->bnqkgd', p.astype(v.dtype), vb)
    return o.reshape(B, S, ATTN_WIDTH)

def conformer_conv(u, conv_w, conv_b, ln_g, ln_b):
    a, b = jnp.split(u, 2, axis=-1)
    g = a * jax.nn.sigmoid(b)
    y = lax.conv_general_dilated(g, conv_w[:, None, :].astype(g.dtype), window_strides=(1,),
                                 padding=[(CONV_KERNEL - 1, 0)],
                                 dimension_numbers=('NWC', 'WIO', 'NWC'),
                                 feature_group_count=CONV_WIDTH)
    y = y + conv_b
    return jax.nn.silu(layer_norm(y, ln_g, ln_b))

def memory_attention(q, mem_k, mem_v):
    s = jnp.einsum('bshd,bmhd->bhsm', q.astype(jnp.float32), mem_k.astype(jnp.float32)) * (MEM_HEAD_DIM ** -0.5)
    p = jax.nn.softmax(s, axis=-1)
    o = jnp.einsum('bhsm,bmhd->bshd', p.astype(mem_v.dtype), mem_v)
    return o.reshape(q.shape[0], q.shape[1], MEM_WIDTH)

def setup_inputs(seed: int = 0) -> dict:
    key = jax.random.key(seed)
    ks = jax.random.split(key, 16)
    f32 = jnp.float32
    n = lambda k, shape, scale: (jax.random.normal(k, shape, f32) * scale)
    return {
        "x": n(ks[0], (BATCH, SEQ, D_MODEL), 1.0),
        "mem": n(ks[1], (BATCH, MEM_LEN, D_MODEL), 1.0),
        "rel_bias": n(ks[2], (NUM_BUCKETS, N_HEADS), 0.5),
        "norm_g": 1.0 + n(ks[3], (DEPTH, D_MODEL), 0.1),
        "w_in": n(ks[4], (DEPTH, D_MODEL, IN_WIDTH), D_MODEL ** -0.5),
        "sinks": n(ks[5], (DEPTH, N_HEADS), 0.5),
        "conv_w": n(ks[6], (DEPTH, CONV_KERNEL, CONV_WIDTH), CONV_KERNEL ** -0.5),
        "conv_b": n(ks[7], (DEPTH, CONV_WIDTH), 0.02),
        "conv_ln_g": 1.0 + n(ks[8], (DEPTH, CONV_WIDTH), 0.1),
        "conv_ln_b": n(ks[9], (DEPTH, CONV_WIDTH), 0.02),
        "mem_norm_g": 1.0 + n(ks[10], (DEPTH, D_MODEL), 0.1),
        "w_mem_kv": n(ks[11], (DEPTH, D_MODEL, 2 * MEM_WIDTH), D_MODEL ** -0.5),
        "w_branch": n(ks[12], (DEPTH, N_BRANCHES, D_MODEL, D_MODEL), D_MODEL ** -0.5),
        "w_out": n(ks[13], (DEPTH, D_MODEL, D_MODEL), D_MODEL ** -0.5),
        "final_norm_g": 1.0 + n(ks[14], (D_MODEL,), 0.1),
    }

def reference(x, mem, rel_bias, norm_g, w_in, sinks, conv_w, conv_b, conv_ln_g, conv_ln_b,
              mem_norm_g, w_mem_kv, w_branch, w_out, final_norm_g):
    B, S = x.shape[0], x.shape[1]
    for l in range(DEPTH):
        h = rms_norm(x, norm_g[l])
        proj = jnp.einsum('bsd,de->bse', h, w_in[l])
        q_a, k_a, v_a, z_a, u_c, z_c, q_m, z_m, g = jnp.split(proj, SPLIT_POINTS, axis=-1)

        o_a = sliding_window_attention(q_a.reshape(B, S, N_HEADS, HEAD_DIM),
                                       k_a.reshape(B, S, N_KV_HEADS, HEAD_DIM),
                                       v_a.reshape(B, S, N_KV_HEADS, HEAD_DIM),
                                       sinks[l], rel_bias) * jax.nn.silu(z_a)

        o_c = conformer_conv(u_c, conv_w[l], conv_b[l], conv_ln_g[l], conv_ln_b[l]) * jax.nn.silu(z_c)

        memn = rms_norm(mem, mem_norm_g[l])
        mk, mv = jnp.split(jnp.einsum('bmd,de->bme', memn, w_mem_kv[l]), 2, axis=-1)
        o_m = memory_attention(q_m.reshape(B, S, MEM_HEADS, MEM_HEAD_DIM),
                               mk.reshape(B, MEM_LEN, MEM_HEADS, MEM_HEAD_DIM),
                               mv.reshape(B, MEM_LEN, MEM_HEADS, MEM_HEAD_DIM)) * jax.nn.silu(z_m)

        o = jnp.stack([o_a, o_c, o_m], axis=2)
        y_br = jnp.einsum('bsnc,ncd->bsnd', o, w_branch[l])
        gates = jax.nn.sigmoid(g.reshape(B, S, N_BRANCHES, D_MODEL))
        y = jnp.sum(gates * y_br, axis=2)
        x = x + jnp.einsum('bsd,de->bse', y, w_out[l])
    return rms_norm(x, final_norm_g)


_drawn_inputs = setup_inputs


def setup_inputs(seed=0):
    import zlib

    import numpy as np

    out = dict(_drawn_inputs(seed))
    spreads = {}
    factors = {'sinks': 64.0,
     'conv_b': 7.571,
     'conv_ln_b': 33.315,
     'mem_norm_g': 8.0,
     'rel_bias': 5.946,
     'conv_ln_g': 5.893}
    for name, (base, spread) in spreads.items():
        noise = np.random.default_rng([zlib.crc32(name.encode()), seed]).standard_normal(out[name].shape)
        drawn = base * np.exp(spread * noise) if base else spread * noise
        out[name] = __import__('jax').numpy.asarray(drawn.astype(out[name].dtype))
    for name, factor in factors.items():
        out[name] = (out[name] * factor).astype(out[name].dtype)
    return out
```

```python
from contextlib import ExitStack

import concourse.bass as bass
from concourse import mybir

ALU = mybir.AluOpType
ACT = mybir.ActivationFunctionType
AX = mybir.AxisListType
F32 = mybir.dt.float32
F32R = mybir.dt.float32r
ds = bass.ds

P = 128
D = 1024
S = 1024
KD = D // P
HALF = 512
NBLK = S // P
HEADS, KV_HEADS, HEAD_DIM = 16, 2, 64
PAIRS = HEADS // 2
PAIRS_PER_KV = PAIRS // KV_HEADS
BUCKETS = 32
WINDOW = 128
TAPS = 31
PAD = TAPS - 1
MEM = 256
MEM_HEADS = 4
RMS_EPS, LN_EPS = 1e-6, 1e-5
MASKED = -1e30

COL_Q, COL_K, COL_V, COL_ZA, COL_A, COL_B = 0, 8, 9, 10, 18, 26
COL_ZC, COL_QM, COL_ZM, COL_G = 34, 42, 50, 58

W_K, W_V, W_AB, W_Q0, W_ZQ = 0, 1, 2, 18, 19
W_M0, W_MLOOP, W_MLAST = 34, 40, 64
W_ZC, W_MERGE, W_OUT = 66, 74, 122
U_M0, U_MLOOP, U_MLAST, U_ZC, U_MERGE = 34, 38, 56, 58, 66
F_M0, F_MLOOP, F_MLAST, F_ZC, F_MERGE = 34, 36, 48, 50, 58
BRANCH_ORDER = (0, 2, 1)
T_A, T_MEMX, T_MV0, T_MLOOP = 16, 80, 84, 85
S_A, S_M, S_LN = 2, 66, 98
O_M, PT_M = 32, 64
V_NORM, V_MEMNORM, V_CONVB, V_LNG, V_LNB = 0, 8, 16, 24, 32
NVEC = 40


class Tally:

    def __init__(self, eng, sem):
        self.eng, self.sem, self.base, self.local = eng, sem, 0, 0

    def tick(self, ins):
        self.local += 1
        return ins.then_inc(self.sem, 1)

    def wait(self):
        self.eng.wait_ge(self.sem, self.base + self.local)

    def loop(self, n, per):
        start = self.base + self.local
        with self.eng.Fori(0, n) as i:
            self.base, self.local = start + i * per, 0
            yield i
            assert self.local == per, (self.local, per)
        self.base, self.local = start + n * per, 0


def build(nc, x, mem, rel_bias, norm_g, w_in, sinks, conv_w, conv_b, conv_ln_g, conv_ln_b,
          mem_norm_g, w_mem_kv, w_branch, w_out, final_norm_g, bucket_onehot, out):
    w_in_v = w_in[0].rearrange("(k p) n -> p k n", p=P)
    w_mem_v = w_mem_kv[0].rearrange("(k p) n -> p k n", p=P)
    w_br_v = w_branch[0].rearrange("b (k p) n -> b p k n", p=P)
    w_out_v = w_out[0].rearrange("(k p) n -> k p n", p=P)
    x_v = x[0].rearrange("(s p) d -> s p d", p=P)
    out_v = out[0].rearrange("(s p) d -> s p d", p=P)

    ROW = 3 * P - 1
    bias_rows = nc.dram_tensor("bias_rows", (HEADS, ROW), F32).ap()
    bias_table = nc.dram_tensor("bias_table", (HEADS, P, 2 * P), F32).ap()
    o_scratch = nc.dram_tensor("o_scratch", (3 * KD, P, S), F32).ap()

    ctx = ExitStack()

    def sb(name, shape, dt=F32, where=ctx):
        return where.enter_context(nc.sbuf_tensor(name, shape, dt))

    def sem(name):
        return ctx.enter_context(nc.semaphore(name))

    def banks(name):
        return ctx.enter_context(nc.psum_tensor(name, [P, 2, HALF], F32))

    with ctx:
        ps_proj, ps_s, ps_t, ps_o = banks("ps_proj"), banks("ps_s"), banks("ps_t"), banks("ps_o")

        hT_hi, hT_lo = sb("hT_hi", [P, KD, S], F32R), sb("hT_lo", [P, KD, S], F32R)
        raw = sb("raw", [P, 2, D])
        w_hi, w_lo = sb("w_hi", [P, 2, KD, P], F32R), sb("w_lo", [P, 2, KD, P], F32R)
        ident = sb("ident", [P, P])
        vec = sb("vec", [P, NVEC])
        small = sb("small", [P, 16])

        early = ExitStack()
        conv = sb("conv", [P, KD + 1, PAD + S], F32, early)
        taps = sb("taps", [P, KD, TAPS], F32, early)
        sink_bc = sb("sink_bc", [P, HEADS], F32, early)
        neg_sink = sb("neg_sink", [P, HEADS], F32, early)
        neg_max = sb("neg_max", [P, NBLK, 2], F32, early)
        row_sum = sb("row_sum", [P, NBLK, 2], F32, early)
        row_max = sb("row_max", [P, NBLK, 2], F32, early)
        sink_arg = sb("sink_arg", [P, NBLK, 2], F32, early)
        sink_exp = sb("sink_exp", [P, NBLK, 2], F32, early)
        inv_sum = sb("inv_sum", [P, NBLK, 2], F32, early)

        st = ExitStack()
        x_nat = sb("x_nat", [P, NBLK, D], F32, st)
        conv_nat = sb("conv_nat", [TAPS, D], F32, st)
        vec_nat = sb("vec_nat", [NVEC, P], F32, st)
        rel_sb = sb("rel_sb", [BUCKETS, HEADS], F32, st)
        onehot_sb = sb("onehot_sb", [BUCKETS, P], F32, st)
        rows_sb = sb("rows_sb", [HEADS, ROW], F32, st)
        st.close()
        st = ExitStack()
        qz_hi = sb("qz_hi", [P, 2, S], F32R, st)
        qz_lo = sb("qz_lo", [P, 2, S], F32R, st)
        kT_hi, kT_lo = sb("kT_hi", [P, S], F32R, st), sb("kT_lo", [P, S], F32R, st)
        v_hi, v_lo = sb("v_hi", [P, NBLK, P], F32R, st), sb("v_lo", [P, NBLK, P], F32R, st)
        prob = sb("prob", [P, NBLK, 2, 2 * P], F32, st)
        pt_hi = sb("pt_hi", [P, 2, HALF], F32R, st)
        pt_lo = sb("pt_lo", [P, 2, HALF], F32R, st)
        th_a = sb("th_a", [P, 2, HALF], F32, st)
        sz_a = sb("sz_a", [P, S], F32, st)
        bias = sb("bias", [P, 2, 2 * P], F32, st)
        st.close()
        st = ExitStack()
        mT_hi, mT_lo = sb("mT_hi", [P, KD, MEM], F32R, st), sb("mT_lo", [P, KD, MEM], F32R, st)
        mk_hi, mk_lo = sb("mk_hi", [P, 2, MEM], F32R, st), sb("mk_lo", [P, 2, MEM], F32R, st)
        mv_hi, mv_lo = sb("mv_hi", [P, 2, MEM], F32R, st), sb("mv_lo", [P, 2, MEM], F32R, st)
        mvT = sb("mvT", [P, 2, MEM], F32, st)
        qm_hi, qm_lo = sb("qm_hi", [P, 2, S], F32R, st), sb("qm_lo", [P, 2, S], F32R, st)
        th_m = sb("th_m", [P, 2, HALF], F32, st)
        sz_m = sb("sz_m", [P, 2, S], F32, st)
        st2 = ExitStack()
        mem_nat = sb("mem_nat", [P, 2, D], F32, st2)
        mem_junk = sb("mem_junk", [P, 2, D], F32, st2)
        st2.close()
        prob_m = sb("prob_m", [P, NBLK, MEM], F32, st)
        ptm_hi = sb("ptm_hi", [P, 2, HALF], F32R, st)
        ptm_lo = sb("ptm_lo", [P, 2, HALF], F32R, st)
        st.close()
        st = ExitStack()
        ln_sum = sb("ln_sum", [P, S], F32, st)
        ln_sq = sb("ln_sq", [P, 2, S], F32, st)
        ln_rstd = sb("ln_rstd", [P, S], F32, st)
        mean_mat = sb("mean_mat", [P, P], F32, st)
        norm_c = sb("norm_c", [P, 2, S], F32, st)
        sz_c = sb("sz_c", [P, 2, S], F32, st)
        st.close()
        early.close()
        oT_hi, oT_lo = sb("oT_hi", [P, KD, S], F32R), sb("oT_lo", [P, KD, S], F32R)
        yT = sb("yT", [P, KD, S])
        gate = sb("gate", [P, S])
        gated_y = sb("gated_y", [P, 2, HALF])
        o_raw = sb("o_raw", [P, 2, S])

        raw_in = [sem("raw_in0"), sem("raw_in1")]
        hi_done, lo_done = sem("hi_done"), sem("lo_done")
        tile_done = sem("tile_done")
        half_done = sem("half_done")
        proj_free = [sem("proj_free0"), sem("proj_free1")]
        const_in = sem("const_in")
        x_in = [sem(f"x_in{i}") for i in range(NBLK)]
        ident_ready = sem("ident_ready")
        vec_t, vec_ready = sem("vec_t"), sem("vec_ready")
        taps_t = sem("taps_t")
        rows_t, rows_ready, table_in = sem("rows_t"), sem("rows_ready"), sem("table_in")
        sumsq, ms_ready, root = sem("sumsq"), sem("ms_ready"), sem("root")
        xn_ready = sem("xn_ready")
        hT_hi_done = sem("hT_hi_done")
        t_ready, t_evac = sem("t_ready"), sem("t_evac")
        values_done = sem("values_done")
        t_hi = sem("t_hi")
        k_hi, v_hi_s = sem("k_hi"), sem("v_hi_s")
        s_ready, s_free = sem("s_ready"), sem("s_free")
        b_sig = sem("b_sig")
        scores_seen = sem("scores_seen")
        q_hi, q_cleared = sem("q_hi"), sem("q_cleared")
        negmax_ready, exp_done = sem("negmax_ready"), sem("exp_done")
        sinkarg_ready, sinkexp_done = sem("sinkarg_ready"), sem("sinkexp_done")
        pn_ready = sem("pn_ready")
        th_done = sem("th_done")
        o_free = sem("o_free")
        c_tile = sem("c_tile")
        scratch = sem("scratch")
        c_stored = [sem("c_stored0"), sem("c_stored1")]
        bias_in = sem("bias_in")
        mem_in, mem_sumsq, mem_ms, mem_root = sem("mem_in"), sem("mem_sumsq"), sem("mem_ms"), sem("mem_root")
        mem_n = sem("mem_n")
        mk_hi_s = sem("mk_hi_s")
        lnsum_ready, centered, squared, sq_ready = sem("lnsum_ready"), sem("centered"), sem("squared"), sem("sq_ready")
        var_ready, ln_root = sem("var_ready"), sem("ln_root")
        mean_mat_ready = sem("mean_mat_ready")
        c_silu = sem("c_silu")
        o_in = [sem("o_in0"), sem("o_in1")]
        norm_ready = sem("norm_ready")
        oT_hi_done, oT_ready = sem("oT_hi_done"), sem("oT_ready")
        gate_done = [sem("gate_done0"), sem("gate_done1")]
        merged = sem("merged")
        y_hi, y_ready = sem("y_hi"), sem("y_ready")
        fg_in = sem("fg_in")
        out_ready, x2_in = sem("out_ready"), [sem("x2_in0"), sem("x2_in1")]
        resid, out_ss, out_ms, out_root, out_row = sem("resid"), sem("out_ss"), sem("out_ms"), sem("out_root"), sem("out_row")
        stored = [sem("stored0"), sem("stored1")]
        dve_step = sem("dve_step")

        def f32(ap):
            return ap.bitcast(F32)

        block = ctx.enter_context(nc.Block())

        @block.sync
        def _(sp):
            def load_raw(w, p, src):
                if not (isinstance(w, int) and w < 2):
                    sp.wait_ge(lo_done, w - 1)
                dst = raw[:, p, :] if len(src.shape) == 2 else raw[:, p, :].rearrange("p (k n) -> p k n", n=P)
                sp.dma_start(dst, src).then_inc(raw_in[p], 16)

            def cols(t):
                return w_in_v[:, :, ds(t * P, P)]

            for s in range(NBLK):
                sp.dma_start(x_nat[:, s, :], x_v[s]).then_inc(x_in[s], 16)
            load_raw(W_K, 0, cols(COL_K))
            load_raw(W_V, 1, cols(COL_V))
            with sp.Fori(0, KD) as t:
                load_raw(W_AB + 2 * t, 0, cols(COL_A + t))
                load_raw(W_AB + 2 * t + 1, 1, cols(COL_B + t))
            load_raw(W_Q0, 0, cols(COL_Q))
            with sp.Fori(0, PAIRS - 1) as t:
                load_raw(W_ZQ + 2 * t, 1, cols(COL_ZA + t))
                load_raw(W_ZQ + 2 * t + 1, 0, cols(COL_Q + 1 + t))
            load_raw(W_M0 - 1, 1, cols(COL_ZA + PAIRS - 1))

            def head_qkv(w, h):
                for i in range(2):
                    load_raw(w + i, i, cols(COL_QM + 2 * h + i))
                for i in range(2):
                    load_raw(w + 2 + i, i, w_mem_v[:, :, ds((2 * h + i) * P, P)])
                for i in range(2):
                    load_raw(w + 4 + i, i, w_mem_v[:, :, ds(D + (2 * h + i) * P, P)])

            head_qkv(W_M0, 0)
            with sp.Fori(0, MEM_HEADS - 1) as h:
                for i in range(2):
                    load_raw(W_MLOOP + 8 * h + i, i, cols(COL_ZM + 2 * h + i))
                head_qkv(W_MLOOP + 8 * h + 2, h + 1)
            for i in range(2):
                load_raw(W_MLAST + i, i, cols(COL_ZM + 2 * (MEM_HEADS - 1) + i))
            with sp.Fori(0, KD // 2) as j:
                for p in range(2):
                    load_raw(W_ZC + 2 * j + p, p, cols(COL_ZC + 2 * j + p))
            for n, br in enumerate(BRANCH_ORDER):
                with sp.Fori(0, KD) as e:
                    load_raw(W_MERGE + 16 * n + 2 * e, 0, cols(COL_G + KD * br + e))
                    load_raw(W_MERGE + 16 * n + 2 * e + 1, 1, w_br_v[br, :, :, ds(e * P, P)])
            for k in range(KD):
                load_raw(W_OUT + k, k % 2, w_out_v[k])
            for s in range(NBLK):
                sp.wait_ge(lo_done, W_OUT + KD)
                if s >= 2:
                    sp.wait_ge(resid, s - 1)
                sp.dma_start(raw[:, s % 2, :], x_v[s]).then_inc(x2_in[s % 2], 16)

        @block.gpsimd
        def _(pool):
            pool.sem_inc(values_done, 2)
            pool.sem_inc(o_free, 2)
            for row, src in ((V_NORM, norm_g), (V_MEMNORM, mem_norm_g), (V_CONVB, conv_b),
                             (V_LNG, conv_ln_g), (V_LNB, conv_ln_b)):
                pool.dma_start(vec_nat[row:row + KD, :], src[0].rearrange("(k p) -> k p", p=P)).then_inc(const_in, 16)
            pool.dma_start(conv_nat[:, :], conv_w[0]).then_inc(const_in, 16)
            pool.dma_start(rel_sb[:, :], rel_bias).then_inc(const_in, 16)
            pool.dma_start(onehot_sb[:, :], bucket_onehot).then_inc(const_in, 16)
            pool.dma_start(sink_bc[:, :], sinks[0].partition_broadcast(P)).then_inc(const_in, 16)
            nc.gpsimd.memset(ident[:, :], 0.0).then_inc(ident_ready, 1)
            pool.wait_ge(ident_ready, 1)
            nc.gpsimd.affine_select(out=ident[:, :], in_=ident[:, :], compare_op=ALU.not_equal, fill=1.0,
                                    base=0, pattern=[[-1, P]], channel_multiplier=1).then_inc(ident_ready, 1)
            pool.wait_ge(rows_ready, 2)
            pool.dma_start(bias_rows, rows_sb[:, :]).then_inc(scratch, 16)
            pool.wait_ge(scratch, 16)
            toeplitz = bass.AP(bias_rows.tensor, P - 1, [[ROW, HEADS], [-1, P], [1, 2 * P]])
            pool.dma_start(bias_table, toeplitz).then_inc(table_in, 16)
            pool.wait_ge(table_in, 16)

            def load_bias(t):
                pool.dma_start(bias[:, :, :], bias_table[ds(2 * t, 2), :, :].rearrange("h q j -> q h j")).then_inc(bias_in, 16)

            def store_a(t):
                pool.wait_ge(o_free, 2 + 4 * t + 4)
                pool.dma_start(o_scratch[ds(t, 1), :, :].rearrange("a p s -> p (a s)"), sz_a[:, :]).then_inc(scratch, 16)

            load_bias(0)
            with pool.Fori(0, PAIRS - 1) as t:
                pool.wait_ge(s_free, S_A + 8 * t + 8)
                load_bias(t + 1)
                store_a(t)
            store_a(PAIRS - 1)
            pool.wait_ge(scratch, 16 * (1 + PAIRS))
            pool.dma_start(mem_nat[:, :, :], mem[0].rearrange("(c p) d -> p c d", p=P)).then_inc(mem_in, 16)
            with pool.Fori(0, MEM_HEADS) as h:
                pool.wait_ge(o_free, 2 + O_M + 4 * h + 4)
                pool.dma_start(o_scratch[ds(2 * KD + 2 * h, 2), :, :].rearrange("a p s -> p a s"),
                               sz_m[:, :, :]).then_inc(scratch, 16)
            for t in range(KD):
                pool.wait_ge(c_tile, t + 1)
                pool.dma_start(o_scratch[KD + t], norm_c[:, t % 2, :]).then_inc(c_stored[t % 2], 16)
            pool.wait_ge(scratch, 16 * (1 + PAIRS + MEM_HEADS))
            for p in range(2):
                pool.wait_ge(c_stored[p], 16 * (KD // 2))
            for n, br in enumerate(BRANCH_ORDER):
                for k in range(KD):
                    i = n * KD + k
                    if i >= 2:
                        pool.wait_ge(oT_ready, i - 1)
                    pool.dma_start(o_raw[:, i % 2, :], o_scratch[br * KD + k]).then_inc(o_in[i % 2], 16)
            pool.wait_ge(merged, 2 * 2 * KD)
            pool.dma_start(gate[:, :], final_norm_g.partition_broadcast(P)).then_inc(fg_in, 16)
            for s in range(NBLK):
                pool.wait_ge(out_row, s + 1)
                pool.dma_start(out_v[s], o_raw[:, s % 2, :]).then_inc(stored[s % 2], 16)
            for p in range(2):
                pool.wait_ge(stored[p], 16 * (NBLK // 2))

        @block.tensor
        def _(pe):
            mm = nc.tensor.matmul

            def split_product(dst, w_hl, x_hl, start=True, stop=True, **kw):
                mm(dst, w_hl[0], x_hl[0], start=start, stop=False, **kw)
                mm(dst, w_hl[0], x_hl[1], start=False, stop=False, **kw)
                return mm(dst, w_hl[1], x_hl[0], start=False, stop=stop, **kw)

            def project(w, p, use, src=(hT_hi, hT_lo), side=None, released=proj_free):
                i = 0
                for half in range(2):
                    col = slice(half * HALF, (half + 1) * HALF)
                    dst = ps_proj[:, half, :]
                    if not (isinstance(use, int) and use == 0):
                        pe.wait_ge(released[half], use)
                    if half == 0:
                        pe.wait_ge(hi_done, w + 1)
                    for k in range(KD):
                        for part in range(2):
                            mm(dst, w_hi[:, p, k, :], src[part][:, k, col], start=(k == 0 and part == 0), stop=False)
                            if side:
                                side(i)
                            i += 1
                    if half == 0:
                        pe.wait_ge(lo_done, w + 1)
                    for k in range(KD):
                        last = mm(dst, w_lo[:, p, k, :], src[0][:, k, col], start=False, stop=(k == KD - 1))
                        if k == KD - 1:
                            last.then_inc(tile_done if half else half_done, 1)
                        if side:
                            side(i)
                        i += 1

            def project_mem(w, i, use):
                dst = ps_proj[:, i, 0:MEM]
                pe.wait_ge(proj_free[i], use)
                pe.wait_ge(lo_done, w + 1)
                for k in range(KD):
                    last = split_product(dst, (w_hi[:, i, k, :], w_lo[:, i, k, :]),
                                         (mT_hi[:, k, :], mT_lo[:, k, :]), start=(k == 0), stop=(k == KD - 1))
                last.then_inc(tile_done, 1)

            def turn(dst, src, n=P):
                return nc.tensor.transpose(dst, src, ident[0:n, 0:n])

            pe.wait_ge(const_in, 16 * 9)
            pe.wait_ge(ident_ready, 2)
            turn(ps_s[:, 0, 0:NVEC], vec_nat[:, :], NVEC).then_inc(vec_t, 1)
            for k in range(KD):
                last = turn(ps_s[:, 1, k * 32:k * 32 + TAPS], conv_nat[:, k * P:(k + 1) * P], TAPS)
            last.then_inc(taps_t, 1)
            mm(ps_o[0:HEADS, 0, 0:P], rel_sb[:, :], onehot_sb[:, :], start=True, stop=True).then_inc(rows_t, 1)
            for n in range(2 * KD):
                half, k = n // KD, n % KD
                if k == 0:
                    pe.wait_ge(xn_ready, 4 * half + 4)
                if n >= 2:
                    pe.wait_ge(t_evac, n - 1)
                for s in range(4):
                    last = turn(ps_t[:, n % 2, s * P:(s + 1) * P], x_nat[:, 4 * half + s, k * P:(k + 1) * P])
                last.then_inc(t_ready, 1)
            pe.wait_ge(t_evac, 2 * KD)
            project(W_K, 0, 0)
            project(W_V, 1, 1)
            pe.wait_ge(proj_free[1], 2)
            pe.wait_ge(vec_ready, 2)
            for c in range(2):
                for s in range(4):
                    b = 4 * c + s
                    last = turn(ps_s[:, c, s * P:(s + 1) * P], sz_a[:, b * P:(b + 1) * P])
                last.then_inc(s_ready, 1)

            with pe.Fori(0, KD) as t:
                project(W_AB + 2 * t, 0, W_AB + 2 * t)
                project(W_AB + 2 * t + 1, 1, W_AB + 2 * t + 1)

            project(W_Q0, 0, W_Q0)

            def scores(t, b):
                n = S_A + 8 * t + b
                if b == 0:
                    for half in range(2):
                        pe.wait_ge(proj_free[half], W_ZQ + 2 * t)
                pe.wait_ge(s_free, n - 1)
                q = slice(b * P, (b + 1) * P)
                lo_key = max(b - 1, 0) * P
                width = (b + 1) * P - lo_key
                for j in range(2):
                    last = split_product(ps_s[:, b % 2, j * 2 * P + 2 * P - width:(j + 1) * 2 * P],
                                         (qz_hi[:, j, q], qz_lo[:, j, q]),
                                         (kT_hi[:, lo_key:lo_key + width], kT_lo[:, lo_key:lo_key + width]))
                last.then_inc(s_ready, 1)

            def turn_probs(t, b):
                n = T_A + 8 * t + b
                pe.wait_ge(pn_ready, 8 * t + b + 1)
                pe.wait_ge(t_evac, n - 1)
                for part in range(1 if b == 0 else 0, 2):
                    for j in range(2):
                        last = turn(ps_t[:, b % 2, (2 * part + j) * P:(2 * part + j + 1) * P],
                                    prob[:, b, j, part * P:(part + 1) * P])
                last.then_inc(t_ready, 1)

            def values(t, b):
                c = b // 2
                pe.wait_ge(t_evac, T_A + 8 * t + b + 1)
                if b % 2 == 0:
                    pe.wait_ge(o_free, 4 * t + c + 1)
                dst = ps_o[:, c % 2, (b % 2) * 2 * P:(b % 2 + 1) * 2 * P]
                for part in range(1 if b == 0 else 0, 2):
                    key = b - 1 + part
                    cols = slice(part * 2 * P, (part + 1) * 2 * P)
                    last = split_product(dst, (v_hi[:, key, :], v_lo[:, key, :]),
                                         (pt_hi[:, b % 2, cols], pt_lo[:, b % 2, cols]),
                                         start=(part == 0 or b == 0), stop=(part == 1))
                last.then_inc(values_done, 1)

            def pair(g, t, last_pair):
                def side_scores(i):
                    if i % 6 == 5:
                        scores(t, i // 6)

                def side_values(i):
                    if i >= 8 and i % 4 == 0 and (i - 8) // 4 < NBLK:
                        turn_probs(t, (i - 8) // 4)
                    if i >= 15 and i % 4 == 3 and (i - 15) // 4 < NBLK:
                        values(t, (i - 15) // 4)

                project(W_ZQ + 2 * t, 1, W_ZQ + 2 * t, side=side_scores)
                if last_pair:
                    for i in range(48):
                        side_values(i)
                else:
                    project(W_ZQ + 2 * t + 1, 0, W_ZQ + 2 * t + 1, side=side_values)

            for g in range(KV_HEADS):
                with pe.Fori(0, PAIRS_PER_KV - 1) as t4:
                    pair(g, PAIRS_PER_KV * g + t4, False)
                pair(g, PAIRS_PER_KV * g + PAIRS_PER_KV - 1, g == KV_HEADS - 1)

            for n in range(KD // 2):
                pe.wait_ge(mem_n, 2)
                pe.wait_ge(t_evac, T_MEMX + n - 1)
                for kk in range(2):
                    for c in range(2):
                        last = turn(ps_t[:, n % 2, kk * MEM + c * P:kk * MEM + (c + 1) * P],
                                    mem_nat[:, c, (2 * n + kk) * P:(2 * n + kk + 1) * P])
                last.then_inc(t_ready, 1)

            def mem_kv(w, use, t_use):
                pe.wait_ge(t_evac, T_MEMX + KD // 2)
                for i in range(2):
                    project_mem(w + i, i, use)
                for i in range(2):
                    project_mem(w + 2 + i, i, use + 1)
                for i in range(2):
                    pe.wait_ge(proj_free[i], use + 2)
                pe.wait_ge(t_evac, t_use - 1)
                for c in range(2):
                    for i in range(2):
                        last = turn(ps_t[:, 0, c * MEM + i * P:c * MEM + (i + 1) * P], mvT[:, i, c * P:(c + 1) * P])
                last.then_inc(t_ready, 1)

            def mem_scores(h, b):
                if b == 0:
                    for i in range(2):
                        pe.wait_ge(proj_free[i], U_MLOOP + 6 * h)
                pe.wait_ge(exp_done, 8 * PAIRS + 8 * h + b - 1)
                q = slice(b * P, (b + 1) * P)
                for i in range(2):
                    last = split_product(ps_s[:, b % 2, 0:MEM], (qm_hi[:, i, q], qm_lo[:, i, q]),
                                         (mk_hi[:, i, :], mk_lo[:, i, :]), start=(i == 0), stop=(i == 1))
                last.then_inc(s_ready, 1)

            def mem_turn(h, c, t_use, bank):
                pe.wait_ge(pn_ready, 8 * PAIRS + 4 * h + c + 1)
                pe.wait_ge(t_evac, t_use - 1)
                for part in range(2):
                    for i in range(2):
                        last = turn(ps_t[:, bank, part * MEM + i * P:part * MEM + (i + 1) * P],
                                    prob_m[:, 2 * c + i, part * P:(part + 1) * P])
                last.then_inc(t_ready, 1)

            def mem_values(h, c, t_use):
                pe.wait_ge(t_evac, t_use + 1)
                pe.wait_ge(o_free, O_M + 4 * h + c + 1)
                for i in range(2):
                    dst = ps_o[:, c % 2, i * MEM:(i + 1) * MEM]
                    for part in range(2):
                        last = split_product(dst, (mv_hi[:, part, i * P:(i + 1) * P], mv_lo[:, part, i * P:(i + 1) * P]),
                                             (ptm_hi[:, c % 2, part * MEM:(part + 1) * MEM],
                                              ptm_lo[:, c % 2, part * MEM:(part + 1) * MEM]),
                                             start=(part == 0), stop=(part == 1))
                last.then_inc(values_done, 1)

            def mem_head(h, w, use, t_use, last_head):
                def side_scores(first):
                    def side(i):
                        if i % 12 == 11:
                            mem_scores(h, first + i // 12)
                    return side

                def side_values(first):
                    def side(i):
                        for c in range(2):
                            if i == 4 + 20 * c:
                                mem_turn(h, first + c, t_use + first + c, 1 - (first + c) % 2)
                            if i == 14 + 20 * c:
                                mem_values(h, first + c, t_use + first + c)
                    return side

                project(w, 0, use, side=side_scores(0))
                project(w + 1, 1, use + 1, side=side_scores(4))
                if last_head:
                    for first in (0, 2):
                        for i in range(48):
                            side_values(first)(i)
                else:
                    project(w + 2, 0, use + 2, side=side_values(0))
                    project(w + 3, 1, use + 3, side=side_values(2))
                    mem_kv(w + 4, use + 4, t_use + 4)

            project(W_M0, 0, U_M0)
            project(W_M0 + 1, 1, U_M0 + 1)
            mem_kv(W_M0 + 2, U_M0 + 2, T_MV0)
            with pe.Fori(0, MEM_HEADS - 1) as h:
                mem_head(h, W_MLOOP + 8 * h, U_MLOOP + 6 * h, T_MLOOP + 5 * h, False)
            mem_head(MEM_HEADS - 1, W_MLAST, U_MLAST, T_MLOOP + 5 * (MEM_HEADS - 1), True)

            pe.wait_ge(mean_mat_ready, 1)
            pe.wait_ge(exp_done, 8 * (PAIRS + MEM_HEADS))
            pe.wait_ge(lnsum_ready, 1)
            for half in range(2):
                mm(ps_s[:, half, :], mean_mat[:, :], ln_sum[:, half * HALF:(half + 1) * HALF],
                   start=True, stop=True).then_inc(s_ready, 1)
            pe.wait_ge(lnsum_ready, 2)
            for half in range(2):
                mm(ps_s[:, half, :], mean_mat[:, :], ln_sum[:, half * HALF:(half + 1) * HALF],
                   start=True, stop=True).then_inc(s_ready, 1)
            with pe.Fori(0, KD // 2) as j:
                for p in range(2):
                    project(W_ZC + 2 * j + p, p, U_ZC + 2 * j + p)

            for n in range(3):
                with pe.Fori(0, KD) as e:
                    w = W_MERGE + 16 * n + 2 * e
                    project(w, 0, U_MERGE + 8 * n + e)
                    pe.wait_ge(oT_ready, KD * n + KD)
                    project(w + 1, 1, 8 * n + e + 1, src=(oT_hi, oT_lo), released=gate_done)

            out_banks = [ps_proj, ps_s, ps_t, ps_o]

            def out_pass(s, k):
                rows = slice(s * P, (s + 1) * P)
                for half in range(2):
                    cols = slice(half * HALF, (half + 1) * HALF)
                    last = split_product(out_banks[s % 4][:, half, :], (oT_hi[:, k, rows], oT_lo[:, k, rows]),
                                         (hT_hi[:, k, cols], hT_lo[:, k, cols]), start=(k == 0), stop=(k == KD - 1))
                return last

            pe.wait_ge(merged, 2 * 2 * KD)
            for k in range(KD):
                pe.wait_ge(y_ready, k + 1)
                pe.wait_ge(lo_done, W_OUT + k + 1)
                for s in range(4):
                    last = out_pass(s, k)
                    if k == KD - 1:
                        last.then_inc(out_ready, 1)
            for s in range(4, NBLK):
                pe.wait_ge(resid, s - 3)
                for k in range(KD):
                    last = out_pass(s, k)
                last.then_inc(out_ready, 1)

        @block.scalar
        def _(act):
            def copy_hi(dst, src, scale=1.0):
                return nc.scalar.activation(dst, src, ACT.Copy, scale=scale)

            def hi_part(w, p, n):
                act.wait_ge(raw_in[p], 16 * (n + 1))
                if not (isinstance(w, int) and w < 2):
                    act.wait_ge(tile_done, w - 1)
                copy_hi(w_hi[:, p, :, :].rearrange("p k n -> p (k n)"), raw[:, p, :]).then_inc(hi_done, 1)

            def wait_half(half, w, full):
                if half == 0:
                    act.wait_ge(half_done, full + 1)
                else:
                    act.wait_ge(tile_done, w + 1)

            def half_cols(half):
                return slice(half * HALF, (half + 1) * HALF)

            for s in range(NBLK):
                act.wait_ge(x_in[s], 16)
                nc.scalar.activation(hT_hi[:, s, :], x_nat[:, s, :], ACT.Square,
                                     accum_out=small[:, s:s + 1]).then_inc(sumsq, 1)
            act.wait_ge(ms_ready, 1)
            nc.scalar.activation(small[:, 8:16], small[:, 8:16], ACT.Sqrt).then_inc(root, 1)
            hi_part(W_K, 0, 0)
            hi_part(W_V, 1, 0)
            act.wait_ge(vec_ready, 1)
            for n in range(2 * KD):
                half, k = n // KD, n % KD
                act.wait_ge(t_ready, n + 1)
                copy_hi(hT_hi[:, k, half_cols(half)], ps_t[:, n % 2, :],
                        vec[:, V_NORM + k:V_NORM + k + 1]).then_inc(t_hi, 1)
            for half in range(2):
                wait_half(half, W_K, W_K)
                copy_hi(kT_hi[:, half_cols(half)], ps_proj[:, half, :]).then_inc(k_hi, 1)
            hi_part(W_AB, 0, 1)
            for half in range(2):
                wait_half(half, W_V, W_V)
                copy_hi(sz_a[:, half_cols(half)], ps_proj[:, half, :]).then_inc(proj_free[half], 1)
            for c in range(2):
                act.wait_ge(s_ready, c + 1)
                copy_hi(v_hi[:, 4 * c:4 * c + 4, :].rearrange("p b n -> p (b n)"), ps_s[:, c, :]).then_inc(v_hi_s, 1)

            with act.Fori(0, KD) as t:
                hi_part(W_AB + 2 * t + 1, 1, 1 + t)
                for half in range(2):
                    wait_half(half, W_AB + 2 * t, W_AB + 2 * t)
                    copy_hi(conv[:, ds(t + 1, 1), PAD + half * HALF:PAD + (half + 1) * HALF]
                            .rearrange("p a s -> p (a s)"), ps_proj[:, half, :]).then_inc(proj_free[half], 1)
                hi_part(W_AB + 2 * t + 2, 0, 2 + t)
                for half in range(2):
                    wait_half(half, W_AB + 2 * t + 1, W_AB + 2 * t + 1)
                    nc.scalar.activation(th_a[:, half, :], ps_proj[:, half, :], ACT.Sigmoid).then_inc(b_sig, 1)

            def q_hi_part(half, w, g):
                wait_half(half, w, w)
                for j in range(2):
                    last = copy_hi(qz_hi[64 * g:64 * g + 64, j, half_cols(half)],
                                   ps_proj[64 * j:64 * j + 64, half, :], HEAD_DIM ** -0.5)
                last.then_inc(q_hi, 1)

            hi_part(W_ZQ, 1, W_ZQ // 2)
            act.wait_ge(q_cleared, 2)
            for half in range(2):
                q_hi_part(half, W_Q0, 0)

            def pair(g_next, t, last_pair):
                w = W_ZQ + 2 * t

                def block_exp(b):
                    act.wait_ge(negmax_ready, 8 * t + b + 1)
                    first = P if b == 0 else 0
                    for j in range(2):
                        seg = prob[:, b, j, first:]
                        last = nc.scalar.activation(seg, seg, ACT.Exp, bias=neg_max[:, b, j:j + 1],
                                                    accum_out=row_sum[:, b, j:j + 1])
                    last.then_inc(exp_done, 1)

                def tanh_half(half):
                    wait_half(half, w, w)
                    nc.scalar.activation(th_a[:, half, :], ps_proj[:, half, :], ACT.Tanh, scale=0.5).then_inc(th_done, 1)

                def sink(grp):
                    act.wait_ge(sinkarg_ready, 2 * t + grp + 1)
                    nc.scalar.activation(sink_exp[:, 4 * grp:4 * grp + 4, :], sink_arg[:, 4 * grp:4 * grp + 4, :],
                                         ACT.Exp).then_inc(sinkexp_done, 1)

                hi_part(w + 1, 0, W_ZQ // 2 + 1 + t)
                for b in range(NBLK):
                    block_exp(b)
                    if b == 3:
                        sink(0)
                    if b == 4:
                        tanh_half(0)
                sink(1)
                tanh_half(1)
                if not last_pair:
                    hi_part(w + 2, 1, W_ZQ // 2 + 1 + t)
                for b in range(NBLK):
                    n = 8 * t + b
                    act.wait_ge(t_ready, T_A + n + 1)
                    act.wait_ge(values_done, n + 1)
                    first = 2 * P if b == 0 else 0
                    copy_hi(pt_hi[:, b % 2, first:], ps_t[:, b % 2, first:]).then_inc(t_hi, 1)
                    if b == 4 and not last_pair:
                        if g_next == 1 and isinstance(t, int):
                            act.wait_ge(q_cleared, 4)
                        q_hi_part(0, w + 1, g_next)
                if not last_pair:
                    q_hi_part(1, w + 1, g_next)

            for g in range(KV_HEADS):
                with act.Fori(0, PAIRS_PER_KV - 1) as t4:
                    pair(g, PAIRS_PER_KV * g + t4, False)
                pair(g + 1, PAIRS_PER_KV * g + PAIRS_PER_KV - 1, g == KV_HEADS - 1)

            act.wait_ge(mem_in, 16)
            for c in range(2):
                nc.scalar.activation(mem_junk[:, c, :], mem_nat[:, c, :], ACT.Square,
                                     accum_out=small[:, c:c + 1]).then_inc(mem_sumsq, 1)
            act.wait_ge(mem_ms, 1)
            nc.scalar.activation(small[:, 8:10], small[:, 8:10], ACT.Sqrt).then_inc(mem_root, 1)
            for n in range(KD // 2):
                act.wait_ge(t_ready, T_MEMX + n + 1)
                for kk in range(2):
                    k = 2 * n + kk
                    last = copy_hi(mT_hi[:, k, :], ps_t[:, n % 2, kk * MEM:(kk + 1) * MEM],
                                   vec[:, V_MEMNORM + k:V_MEMNORM + k + 1])
                last.then_inc(t_hi, 1)

            def qm_hi_part(i, w, full):
                for half in range(2):
                    wait_half(half, w, full)
                    copy_hi(qm_hi[:, i, half_cols(half)], ps_proj[:, half, :], MEM ** -0.5).then_inc(q_hi, 1)

            def mem_kv(w, n, t_use):
                for i in range(2):
                    hi_part(w + 1 + i, 1 - i, n + i)
                    act.wait_ge(tile_done, w + i + 1)
                    copy_hi(mk_hi[:, i, :], ps_proj[:, i, 0:MEM]).then_inc(mk_hi_s, 1)
                for i in range(2):
                    hi_part(w + 3 + i, 1 - i, n + 1 + i)
                    act.wait_ge(tile_done, w + 2 + i + 1)
                    copy_hi(mvT[:, i, :], ps_proj[:, i, 0:MEM]).then_inc(proj_free[i], 1)
                act.wait_ge(t_ready, t_use + 1)
                copy_hi(mv_hi[:, :, :].rearrange("p c n -> p (c n)"), ps_t[:, 0, :]).then_inc(t_hi, 1)

            def mem_head(h, w, full, t_use, n, last_head):
                def block_exp(b):
                    act.wait_ge(negmax_ready, 8 * PAIRS + 8 * h + b + 1)
                    nc.scalar.activation(prob_m[:, b, :], ps_s[:, b % 2, 0:MEM], ACT.Exp, bias=neg_max[:, b, 0:1],
                                         accum_out=row_sum[:, b, 0:1]).then_inc(exp_done, 1)

                def tanh_half(i, half):
                    wait_half(half, w + i, full + i)
                    nc.scalar.activation(th_m[:, half, :], ps_proj[:, half, :], ACT.Tanh, scale=0.5).then_inc(th_done, 1)

                for i in range(2):
                    hi_part(w + 1 + i, 1 - i, n + i)
                    for b in range(4):
                        block_exp(4 * i + b)
                        if b == 2:
                            tanh_half(i, 0)
                    tanh_half(i, 1)
                for i in range(2):
                    if not last_head:
                        hi_part(w + 3 + i, 1 - i, n + 1 + i)
                    for c in (2 * i, 2 * i + 1):
                        act.wait_ge(t_ready, t_use + c + 1)
                        act.wait_ge(values_done, PT_M + 4 * h + c + 1)
                        copy_hi(ptm_hi[:, c % 2, :], ps_t[:, 1 - c % 2, :]).then_inc(t_hi, 1)
                    if not last_head:
                        qm_hi_part(i, w + 2 + i, full + 2 + i)
                if not last_head:
                    mem_kv(w + 4, n + 2, t_use + 4)

            for i in range(2):
                hi_part(W_M0 + 1 + i, 1 - i, W_M0 // 2 + i)
                qm_hi_part(i, W_M0 + i, F_M0 + i)
            mem_kv(W_M0 + 2, W_M0 // 2 + 1, T_MV0)
            with act.Fori(0, MEM_HEADS - 1) as h:
                mem_head(h, W_MLOOP + 8 * h, F_MLOOP + 4 * h, T_MLOOP + 5 * h, W_MLOOP // 2 + 4 * h, False)
            mem_head(MEM_HEADS - 1, W_MLAST, F_MLAST, T_MLOOP + 5 * (MEM_HEADS - 1), W_MLAST // 2, True)

            for t in range(KD):
                act.wait_ge(centered, t + 1)
                if t >= 2:
                    act.wait_ge(squared, t - 1)
                nc.scalar.activation(ln_sq[:, t % 2, :], conv[:, t, PAD:], ACT.Square).then_inc(sq_ready, 1)
            act.wait_ge(var_ready, 1)
            nc.scalar.activation(ln_rstd[:, :], ln_rstd[:, :], ACT.Sqrt).then_inc(ln_root, 1)

            def conv_tiles(j, first):
                for p in range(2):
                    t = 2 * j + p
                    hi_part(W_ZC + 1 + t, 1 - p, (W_ZC + 1 + p) // 2 + j)
                    if not first:
                        act.wait_ge(c_tile, t - 1)
                    for half in range(2):
                        wait_half(half, W_ZC + t, F_ZC + t)
                        nc.scalar.activation(sz_c[:, p, half_cols(half)], ps_proj[:, half, :],
                                             ACT.Silu).then_inc(proj_free[half], 1)
                    act.wait_ge(norm_ready, t + 1)
                    nc.scalar.activation(norm_c[:, p, :], norm_c[:, p, :], ACT.Silu, scale=vec[:, ds(V_LNG + t, 1)],
                                         bias=vec[:, ds(V_LNB + t, 1)]).then_inc(c_silu, 1)

            conv_tiles(0, True)
            with act.Fori(1, KD // 2) as j:
                conv_tiles(j, False)

            def o_hi(i):
                act.wait_ge(o_in[i % 2], 16 * (i // 2 + 1))
                n, k = i // KD, i % KD
                if n > 0:
                    act.wait_ge(tile_done, W_MERGE + 16 * n)
                copy_hi(oT_hi[:, k, :], o_raw[:, i % 2, :]).then_inc(oT_hi_done, 1)

            def merge_step(n, e, last_step):
                w, full = W_MERGE + 16 * n + 2 * e, F_MERGE + 16 * n + 2 * e
                hi_part(w + 1, 1, W_MERGE // 2 + 8 * n + e)
                for half in range(2):
                    wait_half(half, w, full)
                    nc.scalar.activation(gate[:, half_cols(half)], ps_proj[:, half, :],
                                         ACT.Sigmoid).then_inc(gate_done[half], 1)
                if not last_step:
                    hi_part(w + 2, 0, W_MERGE // 2 + 8 * n + e + 1)

            for n in range(3):
                for k in range(KD):
                    o_hi(KD * n + k)
                with act.Fori(0, KD - 1) as e:
                    merge_step(n, e, False)
                merge_step(n, KD - 1, n == 2)

            act.wait_ge(tile_done, W_OUT)
            for k in range(KD):
                act.wait_ge(raw_in[k % 2], 16 * (W_OUT // 2 + k // 2 + 1))
                copy_hi(hT_hi[:, k, :], raw[:, k % 2, :]).then_inc(hi_done, 1)
                act.wait_ge(merged, 2 * 2 * KD)
                copy_hi(oT_hi[:, k, :], yT[:, k, :]).then_inc(y_hi, 1)
            act.wait_ge(y_ready, KD)
            for s in range(NBLK):
                act.wait_ge(resid, s + 1)
                nc.scalar.activation(yT[:, s, :], o_raw[:, s % 2, :], ACT.Square,
                                     accum_out=small[:, s:s + 1]).then_inc(out_ss, 1)
                act.wait_ge(out_ms, s + 1)
                nc.scalar.activation(small[:, 8 + s:9 + s], small[:, 8 + s:9 + s], ACT.Sqrt).then_inc(out_root, 1)

        @block.vector
        def _(dve):
            steps = Tally(dve, dve_step)
            v = nc.vector

            def lo_part(w, p):
                dve.wait_ge(hi_done, w + 1)
                v.tensor_tensor(w_lo[:, p, :, :].rearrange("p k n -> p (k n)"), raw[:, p, :],
                                f32(w_hi[:, p, :, :]).rearrange("p k n -> p (k n)"), ALU.subtract).then_inc(lo_done, 1)

            def rest(dst, src, hi, scale=1.0):
                return v.scalar_tensor_tensor(out=dst, in0=src, scalar=scale, in1=f32(hi),
                                              op0=ALU.mult, op1=ALU.subtract)

            def wait_half(half, w, full):
                if half == 0:
                    dve.wait_ge(half_done, full + 1)
                else:
                    dve.wait_ge(tile_done, w + 1)

            def half_cols(half):
                return slice(half * HALF, (half + 1) * HALF)

            def flat(ap):
                return ap.rearrange("p a s -> p (a s)")

            def tap(c, k, first=False):
                y = flat(conv[:, ds(c, 1), PAD:])
                g = flat(conv[:, ds(c + 1, 1), ds(k, S)])
                w = flat(taps[:, ds(c, 1), ds(k, 1)])
                steps.wait()
                if first:
                    steps.tick(v.tensor_scalar(y, g, w, vec[:, ds(V_CONVB + c, 1)], ALU.mult, ALU.add))
                else:
                    steps.tick(v.scalar_tensor_tensor(out=y, in0=g, scalar=w, in1=y, op0=ALU.mult, op1=ALU.add))

            for c in range(KD + 1):
                steps.tick(v.memset(conv[:, c, 0:PAD], 0.0))
            v.memset(rows_sb[:, :], MASKED).then_inc(rows_ready, 1)
            dve.wait_ge(vec_t, 1)
            v.tensor_copy(vec[:, :], ps_s[:, 0, 0:NVEC]).then_inc(vec_ready, 1)
            dve.wait_ge(taps_t, 1)
            v.tensor_copy(taps[:, :, :], ps_s[:, 1, 0:KD * 32].rearrange("p (k t) -> p k t", t=32)[:, :, 0:TAPS]).then_inc(vec_ready, 1)
            dve.wait_ge(rows_t, 1)
            dve.wait_ge(rows_ready, 1)
            v.tensor_copy(rows_sb[:, P:2 * P], ps_o[0:HEADS, 0, 0:P]).then_inc(rows_ready, 1)
            steps.tick(v.tensor_scalar(neg_sink[:, :], sink_bc[:, :], -1.0, None, ALU.mult))
            dve.wait_ge(sumsq, NBLK)
            v.tensor_scalar(small[:, 8:16], small[:, 0:8], 1.0 / D, RMS_EPS, ALU.mult, ALU.add).then_inc(ms_ready, 1)
            dve.wait_ge(root, 1)
            steps.tick(v.reciprocal(small[:, 8:16], small[:, 8:16]))
            steps.wait()
            for s in range(NBLK):
                v.tensor_scalar(x_nat[:, s, :], x_nat[:, s, :], small[:, 8 + s:9 + s], None, ALU.mult).then_inc(xn_ready, 1)
            lo_part(W_K, 0)
            lo_part(W_V, 1)
            dve.wait_ge(vec_ready, 2)
            for n in range(2 * KD):
                half, k = n // KD, n % KD
                dve.wait_ge(t_hi, n + 1)
                rest(hT_lo[:, k, half_cols(half)], ps_t[:, n % 2, :], hT_hi[:, k, half_cols(half)],
                     vec[:, V_NORM + k:V_NORM + k + 1]).then_inc(t_evac, 1)
            dve.wait_ge(t_ready, 2 * KD)
            for part in (qz_hi, qz_lo):
                v.memset(f32(part[64:128, :, :]), 0.0).then_inc(q_cleared, 1)
            for half in range(2):
                dve.wait_ge(k_hi, half + 1)
                rest(kT_lo[:, half_cols(half)], ps_proj[:, half, :], kT_hi[:, half_cols(half)]).then_inc(proj_free[half], 1)
            lo_part(W_AB, 0)
            for c in range(2):
                dve.wait_ge(v_hi_s, c + 1)
                rest(v_lo[:, 4 * c:4 * c + 4, :].rearrange("p b n -> p (b n)"), ps_s[:, c, :],
                     v_hi[:, 4 * c:4 * c + 4, :].rearrange("p b n -> p (b n)")).then_inc(s_free, 1)

            def gated(t, half):
                g = flat(conv[:, ds(t + 1, 1), PAD + half * HALF:PAD + (half + 1) * HALF])
                dve.wait_ge(b_sig, 2 * t + half + 1)
                v.tensor_tensor(g, g, th_a[:, half, :], ALU.mult).then_inc(proj_free[half], 1)

            for j in steps.loop(KD // 2, TAPS):
                for p in range(2):
                    t = 2 * j + p
                    todo = list(range(0, 16) if p == 0 else range(16, TAPS))

                    def some(n):
                        for k in todo[:n]:
                            tap(j, k, k == 0)
                        del todo[:n]
                    lo_part(W_AB + 2 * t + 1, 1)
                    if p == 1:
                        some(7)
                    lo_part(W_AB + 2 * t + 2, 0)
                    if p == 1:
                        some(3)
                    gated(t, 0)
                    if p == 1:
                        some(2)
                    gated(t, 1)
                    if p == 0:
                        for half in range(2):
                            dve.wait_ge(proj_free[half], W_AB + 2 * t + 2)
                    some(99)

            def q_lo_part(half, g):
                for jj in range(2):
                    rows, src = slice(64 * g, 64 * g + 64), slice(64 * jj, 64 * jj + 64)
                    last = rest(qz_lo[rows, jj, half_cols(half)], ps_proj[src, half, :],
                                qz_hi[rows, jj, half_cols(half)], HEAD_DIM ** -0.5)
                    if jj == 0:
                        steps.tick(last)
                last.then_inc(proj_free[half], 1)

            def pair(g, g_next, t, last_pair, todo):
                w = W_ZQ + 2 * t

                def some(n):
                    for k in todo[:n]:
                        tap(4 + g, k)
                    del todo[:n]

                def biased(b):
                    first = P if b == 0 else 0
                    dve.wait_ge(s_ready, S_A + 8 * t + b + 1)
                    dve.sem_inc(scores_seen, 1)
                    for j in range(2):
                        last = v.tensor_tensor_reduce(prob[:, b, j, first:], ps_s[:, b % 2, j * 2 * P + first:(j + 1) * 2 * P],
                                                      bias[:, j, first:], 1.0, MASKED, ALU.add, ALU.max, row_max[:, b, j:j + 1])
                        if j == 0:
                            steps.tick(last)
                    last.then_inc(s_free, 1)
                    steps.wait()
                    dve.wait_ge(s_free, S_A + 8 * t + b + 1)
                    v.scalar_tensor_tensor(out=neg_max[:, b, :], in0=row_max[:, b, :], scalar=-1.0,
                                           in1=neg_sink[:, ds(2 * t, 2)], op0=ALU.mult, op1=ALU.min).then_inc(negmax_ready, 1)

                def sink_args(grp):
                    blocks = slice(4 * grp, 4 * grp + 4)
                    dve.wait_ge(negmax_ready, 8 * t + 4 * grp + 4)
                    for j in range(2):
                        last = v.tensor_scalar(sink_arg[:, blocks, j], neg_max[:, blocks, j], sink_bc[:, ds(2 * t + j, 1)],
                                               None, ALU.add)
                        if j == 0:
                            steps.tick(last)
                    last.then_inc(sinkarg_ready, 1)

                def inverses(grp):
                    blocks = slice(4 * grp, 4 * grp + 4)
                    dve.wait_ge(exp_done, 8 * t + 4 * grp + 4)
                    dve.wait_ge(sinkexp_done, 2 * t + grp + 1)
                    steps.tick(v.tensor_tensor(row_sum[:, blocks, :], row_sum[:, blocks, :], sink_exp[:, blocks, :], ALU.add))
                    steps.wait()
                    steps.tick(v.reciprocal(inv_sum[:, blocks, :], row_sum[:, blocks, :]))

                def silu_half(half):
                    dve.wait_ge(th_done, 2 * t + half + 1)
                    dve.wait_ge(scratch, 16 * (1 + t))
                    v.scalar_tensor_tensor(out=sz_a[:, half_cols(half)], in0=th_a[:, half, :], scalar=1.0,
                                           in1=ps_proj[:, half, :], op0=ALU.add, op1=ALU.mult).then_inc(proj_free[half], 1)

                lo_part(w + 1, 0)
                dve.wait_ge(bias_in, 16 * (t + 1))
                dve.wait_ge(t_ready, T_A + 8 * t)
                for b in range(NBLK):
                    biased(b)
                    if b == 3:
                        sink_args(0)
                    if b in (1, 4, 6):
                        some(1)
                    if b == 5:
                        silu_half(0)
                        inverses(0)
                sink_args(1)
                silu_half(1)
                inverses(1)
                if not last_pair:
                    lo_part(w + 2, 1)
                steps.wait()
                for b in range(NBLK + 2):
                    if b < NBLK:
                        first = P if b == 0 else 0
                        for j in range(2):
                            last = v.tensor_scalar(prob[:, b, j, first:], prob[:, b, j, first:], inv_sum[:, b, j:j + 1], 0.5,
                                                   ALU.mult, ALU.mult)
                            if j == 0:
                                steps.tick(last)
                        last.then_inc(pn_ready, 1)
                    if 1 <= b <= NBLK:
                        c = b - 1
                        first = 2 * P if c == 0 else 0
                        dve.wait_ge(t_hi, T_A + 8 * t + c + 1)
                        rest(pt_lo[:, c % 2, first:], ps_t[:, c % 2, first:], pt_hi[:, c % 2, first:]).then_inc(t_evac, 1)
                    if b >= 3 and b % 2 == 1:
                        c = (b - 3) // 2
                        dve.wait_ge(values_done, 2 + 8 * t + 2 * c + 2)
                        if c == 0:
                            dve.wait_ge(proj_free[0], w + 1)
                            dve.wait_ge(proj_free[1], w + 1)
                        for j in range(2):
                            o = sz_a[64 * j:64 * j + 64, 2 * c * P:(2 * c + 2) * P].rearrange("p (b q) -> p b q", q=P)
                            src = ps_o[64 * g:64 * g + 64, c % 2, :].rearrange("p (b h q) -> p b h q", b=2, h=2)[:, :, j, :]
                            last = v.tensor_tensor(o, src, o, ALU.mult)
                            if j == 0:
                                steps.tick(last)
                        last.then_inc(o_free, 1)
                    if b == 5 and not last_pair:
                        if g_next != g:
                            dve.wait_ge(s_ready, S_A + 8 * t + 8)
                            for part in (qz_hi, qz_lo):
                                v.memset(f32(part[0:64, :, :]), 0.0).then_inc(q_cleared, 1)
                        dve.wait_ge(q_hi, 2 * t + 3)
                        q_lo_part(0, g_next)
                    if b == 8:
                        some(99)
                if not last_pair:
                    dve.wait_ge(q_hi, 2 * t + 4)
                    q_lo_part(1, g_next)

            lo_part(W_ZQ, 1)
            for half in range(2):
                dve.wait_ge(q_hi, half + 1)
                q_lo_part(half, 0)
            for g in range(KV_HEADS):
                tap(4 + g, 0, True)
                for t4 in steps.loop(PAIRS_PER_KV - 1, 36):
                    pair(g, g, PAIRS_PER_KV * g + t4, False, [1 + 8 * t4 + i for i in range(8)])
                pair(g, g + 1, PAIRS_PER_KV * g + PAIRS_PER_KV - 1, g == KV_HEADS - 1, list(range(25, TAPS)))

            dve.wait_ge(mem_sumsq, 2)
            v.tensor_scalar(small[:, 8:10], small[:, 0:2], 1.0 / D, RMS_EPS, ALU.mult, ALU.add).then_inc(mem_ms, 1)
            dve.wait_ge(mem_root, 1)
            steps.tick(v.reciprocal(small[:, 8:10], small[:, 8:10]))
            steps.wait()
            for c in range(2):
                v.tensor_scalar(mem_nat[:, c, :], mem_nat[:, c, :], small[:, 8 + c:9 + c], None, ALU.mult).then_inc(mem_n, 1)
            for n in range(KD // 2):
                dve.wait_ge(t_hi, T_MEMX + n + 1)
                for kk in range(2):
                    k = 2 * n + kk
                    last = rest(mT_lo[:, k, :], ps_t[:, n % 2, kk * MEM:(kk + 1) * MEM], mT_hi[:, k, :],
                                vec[:, V_MEMNORM + k:V_MEMNORM + k + 1])
                    if kk == 0:
                        steps.tick(last)
                last.then_inc(t_evac, 1)

            def qm_lo_part(i, n):
                for half in range(2):
                    dve.wait_ge(q_hi, n + half + 1)
                    rest(qm_lo[:, i, half_cols(half)], ps_proj[:, half, :], qm_hi[:, i, half_cols(half)],
                         MEM ** -0.5).then_inc(proj_free[half], 1)

            def mem_kv(w, heads_before, t_use):
                for i in range(2):
                    lo_part(w + 1 + i, 1 - i)
                    dve.wait_ge(mk_hi_s, 2 * heads_before + i + 1)
                    rest(mk_lo[:, i, :], ps_proj[:, i, 0:MEM], mk_hi[:, i, :]).then_inc(proj_free[i], 1)
                for i in range(2):
                    lo_part(w + 3 + i, 1 - i)
                dve.wait_ge(t_hi, t_use + 1)
                rest(flat(mv_lo[:, :, :]), ps_t[:, 0, :], flat(mv_hi[:, :, :])).then_inc(t_evac, 1)

            def mem_head(h, w, t_use, last_head, todo):
                def some(n):
                    for k in todo[:n]:
                        tap(7, k)
                    del todo[:n]

                def maximum(b):
                    dve.wait_ge(s_ready, S_M + 8 * h + b + 1)
                    steps.tick(v.tensor_reduce(row_max[:, b, 0:1], ps_s[:, b % 2, 0:MEM], AX.X, ALU.max))
                    steps.wait()
                    v.tensor_scalar(neg_max[:, b, 0:1], row_max[:, b, 0:1], -1.0, None, ALU.mult).then_inc(negmax_ready, 1)

                def silu_half(i, half):
                    dve.wait_ge(th_done, 2 * PAIRS + 4 * h + 2 * i + half + 1)
                    dve.wait_ge(scratch, 16 * (1 + PAIRS + h))
                    v.scalar_tensor_tensor(out=sz_m[:, i, half_cols(half)], in0=th_m[:, half, :], scalar=1.0,
                                           in1=ps_proj[:, half, :], op0=ALU.add, op1=ALU.mult).then_inc(proj_free[half], 1)

                for i in range(2):
                    lo_part(w + 1 + i, 1 - i)
                    for b in range(4):
                        maximum(4 * i + b)
                        if b in (0, 1):
                            some(1)
                    silu_half(i, 0)
                    dve.wait_ge(exp_done, 8 * PAIRS + 8 * h + 4 * i + 4)
                    steps.tick(v.reciprocal(inv_sum[:, 4 * i:4 * i + 4, 0:1], row_sum[:, 4 * i:4 * i + 4, 0:1]))
                    silu_half(i, 1)
                steps.wait()
                for i in range(2):
                    if not last_head:
                        lo_part(w + 3 + i, 1 - i)
                    for c in (2 * i, 2 * i + 1):
                        for b in (2 * c, 2 * c + 1):
                            last = v.tensor_scalar(prob_m[:, b, :], prob_m[:, b, :], inv_sum[:, b, 0:1], 0.5, ALU.mult, ALU.mult)
                            if b % 2 == 0:
                                steps.tick(last)
                        last.then_inc(pn_ready, 1)
                        some(1)
                        dve.wait_ge(t_hi, t_use + c + 1)
                        rest(ptm_lo[:, c % 2, :], ps_t[:, 1 - c % 2, :], ptm_hi[:, c % 2, :]).then_inc(t_evac, 1)
                        some(1)
                        dve.wait_ge(values_done, 2 + PT_M + 4 * h + c + 1)
                        o = sz_m[:, :, 2 * c * P:(2 * c + 2) * P]
                        v.tensor_tensor(o, ps_o[:, c % 2, :].rearrange("p (i q) -> p i q", i=2), o, ALU.mult).then_inc(o_free, 1)
                    if not last_head:
                        qm_lo_part(i, 2 * PAIRS + 4 * h + 4 + 2 * i)
                some(99)
                if not last_head:
                    mem_kv(w + 4, h + 1, t_use + 4)

            for i in range(2):
                lo_part(W_M0 + 1 + i, 1 - i)
                qm_lo_part(i, 2 * PAIRS + 2 * i)
            mem_kv(W_M0 + 2, 0, T_MV0)
            for k in range(TAPS):
                tap(6, k, k == 0)
            tap(7, 0, True)
            for h in steps.loop(MEM_HEADS - 1, 24):
                mem_head(h, W_MLOOP + 8 * h, T_MLOOP + 5 * h, False, [1 + 10 * h + i for i in range(10)])
            mem_head(MEM_HEADS - 1, W_MLAST, T_MLOOP + 5 * (MEM_HEADS - 1), True, [])

            v.memset(mean_mat[:, :], 1.0 / D).then_inc(mean_mat_ready, 1)
            dve.wait_ge(scratch, 16 * (1 + PAIRS + MEM_HEADS))
            y0, y1 = conv[:, 0, PAD:], conv[:, 1, PAD:]
            steps.wait()
            steps.tick(v.tensor_tensor(ln_sum[:, :], y0, y1, ALU.add))
            for t in range(2, KD):
                steps.wait()
                last = v.tensor_tensor(ln_sum[:, :], ln_sum[:, :], conv[:, t, PAD:], ALU.add)
                if t < KD - 1:
                    steps.tick(last)
            last.then_inc(lnsum_ready, 1)
            dve.wait_ge(s_ready, S_LN + 2)
            mean = ps_s[:, :, :].rearrange("p h s -> p (h s)")
            for t in range(KD):
                y = conv[:, t, PAD:]
                v.tensor_tensor(y, y, mean, ALU.subtract).then_inc(centered, 1)
            for t in range(KD):
                dve.wait_ge(sq_ready, t + 1)
                if t == 0:
                    v.tensor_copy(ln_sum[:, :], ln_sq[:, 0, :]).then_inc(squared, 1)
                else:
                    dve.wait_ge(squared, t)
                    last = v.tensor_tensor(ln_sum[:, :], ln_sum[:, :], ln_sq[:, t % 2, :], ALU.add)
                    last.then_inc(squared if t < KD - 1 else lnsum_ready, 1)
            dve.wait_ge(s_ready, S_LN + 4)
            v.tensor_scalar(ln_rstd[:, :], mean, LN_EPS, None, ALU.add).then_inc(var_ready, 1)
            dve.wait_ge(ln_root, 1)
            steps.tick(v.reciprocal(ln_rstd[:, :], ln_rstd[:, :]))
            steps.wait()

            def conv_tiles(j, first):
                for p in range(2):
                    t = 2 * j + p
                    lo_part(W_ZC + 1 + t, 1 - p)
                    if not first:
                        dve.wait_ge(c_stored[p], 16 * j)
                    v.tensor_tensor(norm_c[:, p, :], flat(conv[:, ds(t, 1), PAD:]), ln_rstd[:, :], ALU.mult).then_inc(norm_ready, 1)
                    dve.wait_ge(c_silu, t + 1)
                    for half in range(2):
                        dve.wait_ge(proj_free[half], U_ZC + t + 1)
                    v.tensor_tensor(norm_c[:, p, :], norm_c[:, p, :], sz_c[:, p, :], ALU.mult).then_inc(c_tile, 1)

            conv_tiles(0, True)
            with dve.Fori(1, KD // 2) as j:
                conv_tiles(j, False)

            def merge_half(n, e, half):
                w, full = W_MERGE + 16 * n + 2 * e + 1, F_MERGE + 16 * n + 2 * e + 1
                wait_half(half, w, full)
                dve.wait_ge(gate_done[half], 8 * n + e + 1)
                y = flat(yT[:, ds(e, 1), half_cols(half)])
                if n == 0:
                    v.tensor_tensor(y, ps_proj[:, half, :], gate[:, half_cols(half)], ALU.mult).then_inc(proj_free[half], 1)
                else:
                    v.tensor_tensor(gated_y[:, half, :], ps_proj[:, half, :], gate[:, half_cols(half)],
                                    ALU.mult).then_inc(proj_free[half], 1)
                    dve.wait_ge(proj_free[half], U_MERGE + 8 * n + e + 1)
                    last = v.tensor_tensor(y, y, gated_y[:, half, :], ALU.add)
                    last.then_inc(merged, 1)

            def merge_step(n, e, last_step):
                w = W_MERGE + 16 * n + 2 * e
                lo_part(w + 1, 1)
                if not last_step:
                    lo_part(w + 2, 0)
                for half in range(2):
                    merge_half(n, e, half)

            for n in range(3):
                for k in range(KD):
                    i = KD * n + k
                    dve.wait_ge(oT_hi_done, i + 1)
                    v.tensor_tensor(oT_lo[:, k, :], o_raw[:, i % 2, :], f32(oT_hi[:, k, :]), ALU.subtract).then_inc(oT_ready, 1)
                with dve.Fori(0, KD - 1) as e:
                    merge_step(n, e, False)
                merge_step(n, KD - 1, n == 2)

            for k in range(KD):
                dve.wait_ge(hi_done, W_OUT + k + 1)
                v.tensor_tensor(hT_lo[:, k, :], raw[:, k % 2, :], f32(hT_hi[:, k, :]), ALU.subtract).then_inc(lo_done, 1)
                dve.wait_ge(y_hi, k + 1)
                v.tensor_tensor(oT_lo[:, k, :], yT[:, k, :], f32(oT_hi[:, k, :]), ALU.subtract).then_inc(y_ready, 1)
            dve.wait_ge(oT_ready, 3 * KD)
            banks_of = [ps_proj, ps_s, ps_t, ps_o]

            def residual(s):
                dve.wait_ge(out_ready, s + 1)
                dve.wait_ge(x2_in[s % 2], 16 * (s // 2 + 1))
                if s >= 2:
                    dve.wait_ge(stored[s % 2], 16 * (s // 2))
                v.tensor_tensor(o_raw[:, s % 2, :], banks_of[s % 4][:, :, :].rearrange("p h s -> p (h s)"),
                                raw[:, s % 2, :], ALU.add).then_inc(resid, 1)

            def finish(s):
                dve.wait_ge(out_ss, s + 1)
                v.tensor_scalar(small[:, 8 + s:9 + s], small[:, s:s + 1], 1.0 / D, RMS_EPS, ALU.mult, ALU.add).then_inc(out_ms, 1)
                dve.wait_ge(out_root, s + 1)
                steps.tick(v.reciprocal(small[:, 8 + s:9 + s], small[:, 8 + s:9 + s]))
                steps.wait()
                dve.wait_ge(fg_in, 16)
                v.scalar_tensor_tensor(out=o_raw[:, s % 2, :], in0=o_raw[:, s % 2, :], scalar=small[:, 8 + s:9 + s],
                                       in1=gate[:, :], op0=ALU.mult, op1=ALU.mult).then_inc(out_row, 1)

            for s in range(NBLK):
                residual(s)
                finish(s)


def bucket_of_distance(n):
    import math
    exact = BUCKETS // 2
    if n < exact:
        return n
    return min(exact + int(math.log(n / exact) / math.log(WINDOW / exact) * (BUCKETS - exact)), BUCKETS - 1)


_INS = ["x", "mem", "rel_bias", "norm_g", "w_in", "sinks", "conv_w", "conv_b", "conv_ln_g", "conv_ln_b",
        "mem_norm_g", "w_mem_kv", "w_branch", "w_out", "final_norm_g"]


def kernel(**inputs):
    import numpy as np
    import concourse.bacc as bacc
    from concourse.bass_utils import run_bass_kernel_spmd

    nc = bacc.Bacc("TRN2", target_bir_lowering=False, num_devices=1)
    arrays, args = {}, []
    onehot = np.zeros((BUCKETS, WINDOW), np.float32)
    for u in range(WINDOW):
        onehot[bucket_of_distance(WINDOW - 1 - u), u] = 1.0
    for name in _INS + ["bucket_onehot"]:
        a = onehot if name == "bucket_onehot" else np.ascontiguousarray(inputs[name])
        arrays[f"in_{name}"] = a
        args.append(nc.dram_tensor(f"in_{name}", a.shape, mybir.dt.from_np(a.dtype), kind="ExternalInput").ap())
    out = nc.dram_tensor("out", (1, S, D), F32, kind="ExternalOutput").ap()
    build(nc, *args, out)
    r = run_bass_kernel_spmd(nc, [arrays], core_ids=[0])
    return r.results[0]["out"]
```

```python
from contextlib import ExitStack

import concourse.bass as bass
from concourse import mybir

ALU = mybir.AluOpType
ACT = mybir.ActivationFunctionType
AX = mybir.AxisListType
F32 = mybir.dt.float32
F32R = mybir.dt.float32r
ds = bass.ds

P = 128
D = 1024
S = 1024
KD = D // P
HALF = 512
NBLK = S // P
HEADS, KV_HEADS, HEAD_DIM = 16, 2, 64
PAIRS = HEADS // 2
PAIRS_PER_KV = PAIRS // KV_HEADS
BUCKETS = 32
WINDOW = 128
TAPS = 31
PAD = TAPS - 1
MEM = 256
MEM_HEADS = 4
RMS_EPS, LN_EPS = 1e-6, 1e-5
MASKED = -1e30

COL_Q, COL_K, COL_V, COL_ZA, COL_A, COL_B = 0, 8, 9, 10, 18, 26
COL_ZC, COL_QM, COL_ZM, COL_G = 34, 42, 50, 58

W_K, W_V, W_AB, W_Q0, W_ZQ = 0, 1, 2, 18, 19
W_M0, W_MLOOP, W_MLAST = 34, 40, 64
W_ZC, W_MERGE, W_OUT = 66, 74, 122
U_M0, U_MLOOP, U_MLAST, U_ZC, U_MERGE = 34, 38, 56, 58, 66
F_M0, F_MLOOP, F_MLAST, F_ZC, F_MERGE = 34, 36, 48, 50, 58
BRANCH_ORDER = (1, 0, 2)
T_MEMX, T_A, T_MV0, T_MLOOP = 16, 20, 84, 85
S_A, S_M, S_LN = 2, 66, 98
ZC_SLOTS, RAW_SLOTS = 3, 4
NORMS_ACT = 4
PAIR_STEPS = 25
HEAD_STEPS = 10
NORM_GROUPS = (range(0, 4), range(4, 8), range(8, 10))
MS = 16
O_M, PT_M = 32, 64
V_NORM, V_MEMNORM, V_CONVB, V_LNG, V_LNB = 0, 8, 16, 24, 32
NVEC = 40


class Tally:

    def __init__(self, eng, sem):
        self.eng, self.sem, self.base, self.local = eng, sem, 0, 0

    def tick(self, ins):
        self.local += 1
        return ins.then_inc(self.sem, 1)

    def wait(self):
        self.eng.wait_ge(self.sem, self.base + self.local)

    def loop(self, n, per):
        start = self.base + self.local
        with self.eng.Fori(0, n) as i:
            self.base, self.local = start + i * per, 0
            yield i
            assert self.local == per, (self.local, per)
        self.base, self.local = start + n * per, 0


def build(nc, x, mem, rel_bias, norm_g, w_in, sinks, conv_w, conv_b, conv_ln_g, conv_ln_b,
          mem_norm_g, w_mem_kv, w_branch, w_out, final_norm_g, bucket_onehot, out):
    w_in_v = w_in[0].rearrange("(k p) n -> p k n", p=P)
    w_mem_v = w_mem_kv[0].rearrange("(k p) n -> p k n", p=P)
    w_br_v = w_branch[0].rearrange("b (k p) n -> b p k n", p=P)
    w_out_v = w_out[0].rearrange("(k p) n -> k p n", p=P)
    x_v = x[0].rearrange("(s p) d -> s p d", p=P)
    out_v = out[0].rearrange("(s p) d -> s p d", p=P)

    ROW = 3 * P - 1
    bias_rows = nc.dram_tensor("bias_rows", (HEADS, ROW), F32).ap()
    bias_table = nc.dram_tensor("bias_table", (HEADS, P, 2 * P), F32).ap()
    o_scratch = nc.dram_tensor("o_scratch", (2 * KD, P, S), F32).ap()

    ctx = ExitStack()

    def sb(name, shape, dt=F32, where=ctx):
        return where.enter_context(nc.sbuf_tensor(name, shape, dt))

    def sem(name):
        return ctx.enter_context(nc.semaphore(name))

    def banks(name):
        return ctx.enter_context(nc.psum_tensor(name, [P, 2, HALF], F32))

    with ctx:
        ps_proj, ps_s, ps_t, ps_o = banks("ps_proj"), banks("ps_s"), banks("ps_t"), banks("ps_o")

        hT_hi, hT_lo = sb("hT_hi", [P, KD, S], F32R), sb("hT_lo", [P, KD, S], F32R)
        raw = sb("raw", [P, 2, D])
        w_hi, w_lo = sb("w_hi", [P, 2, KD, P], F32R), sb("w_lo", [P, 2, KD, P], F32R)
        ident = sb("ident", [P, P])
        mean_mat = sb("mean_mat", [P, P])
        vec = sb("vec", [P, NVEC])
        sums = sb("sums", [P, 2 * MS])

        conv = sb("conv", [P, KD + 1, PAD + S], F32)
        taps = sb("taps", [P, KD, TAPS], F32)
        sink_bc = sb("sink_bc", [P, HEADS], F32)
        neg_sink = sb("neg_sink", [P, HEADS], F32)
        neg_max = sb("neg_max", [P, NBLK, 2], F32)
        row_sum = sb("row_sum", [P, NBLK, 2], F32)
        row_max = sb("row_max", [P, NBLK, 2], F32)
        sink_arg = sb("sink_arg", [P, NBLK, 2], F32)
        sink_exp = sb("sink_exp", [P, NBLK, 2], F32)
        inv_sum = sb("inv_sum", [P, NBLK, 2], F32)

        mid = ExitStack()
        mT_hi, mT_lo = sb("mT_hi", [P, KD, MEM], F32R, mid), sb("mT_lo", [P, KD, MEM], F32R, mid)

        st = ExitStack()
        unused_squares = sb("unused_squares", [P, D], F32, st)
        mem_nat = sb("mem_nat", [P, 2, D], F32, st)
        x_nat = sb("x_nat", [P, NBLK, D], F32, st)
        conv_nat = sb("conv_nat", [TAPS, D], F32, st)
        vec_nat = sb("vec_nat", [NVEC, P], F32, st)
        rel_sb = sb("rel_sb", [BUCKETS, HEADS], F32, st)
        onehot_sb = sb("onehot_sb", [BUCKETS, P], F32, st)
        rows_sb = sb("rows_sb", [HEADS, ROW], F32, st)
        st.close()
        st = ExitStack()
        qz_hi = sb("qz_hi", [P, 2, S], F32R, st)
        qz_lo = sb("qz_lo", [P, 2, S], F32R, st)
        kT_hi, kT_lo = sb("kT_hi", [P, S], F32R, st), sb("kT_lo", [P, S], F32R, st)
        v_hi, v_lo = sb("v_hi", [P, NBLK, P], F32R, st), sb("v_lo", [P, NBLK, P], F32R, st)
        prob = sb("prob", [P, NBLK, 2, 2 * P], F32, st)
        pt_hi = sb("pt_hi", [P, 2, HALF], F32R, st)
        pt_lo = sb("pt_lo", [P, 2, HALF], F32R, st)
        sz_a = sb("sz_a", [P, S], F32, st)
        th_a = sz_a[:, :].rearrange("p (h s) -> p h s", h=2)
        bias = sb("bias", [P, 2, 2 * P], F32, st)
        st.close()
        st = ExitStack()
        qm_hi = sb("qm_hi", [P, 2, S], F32R, st)
        qm_lo = sb("qm_lo", [P, 2, S], F32R, st)
        mk_hi, mk_lo = sb("mk_hi", [P, 2, MEM], F32R, st), sb("mk_lo", [P, 2, MEM], F32R, st)
        mv_hi, mv_lo = sb("mv_hi", [P, 2, MEM], F32R, st), sb("mv_lo", [P, 2, MEM], F32R, st)
        th_m = sb("th_m", [P, 2, HALF], F32, st)
        sz_m = sb("sz_m", [P, 2, S], F32, st)
        prob_m = sb("prob_m", [P, NBLK, MEM], F32, st)
        ptm_hi = sb("ptm_hi", [P, 2, HALF], F32R, st)
        ptm_lo = sb("ptm_lo", [P, 2, HALF], F32R, st)
        late_tiles = sb("late_tiles", [P, 2, S], F32, st)
        mvT = sb("mvT", [P, 2, MEM], F32, st)
        st.close()
        mid.close()
        st = ExitStack()
        ln_sum = sb("ln_sum", [P, S], F32, st)
        ln_sq = sb("ln_sq", [P, 2, S], F32, st)
        st.close()
        oT_hi, oT_lo = sb("oT_hi", [P, KD, S], F32R), sb("oT_lo", [P, KD, S], F32R)
        st = ExitStack()
        rstd_diag = sb("rstd_diag", [P, NBLK, P], F32, st)
        sz_c = sb("sz_c", [P, ZC_SLOTS, S], F32, st)
        st.close()
        yT, gate = conv[:, 0:KD, PAD:], conv[:, KD, PAD:]
        o_raw = sb("o_raw", [P, RAW_SLOTS, S])

        raw_in = [sem("raw_in0"), sem("raw_in1")]
        hi_done, lo_done = sem("hi_done"), sem("lo_done")
        tile_done = sem("tile_done")
        half_done = sem("half_done")
        proj_free = [sem("proj_free0"), sem("proj_free1")]
        vec_in, const_in = sem("vec_in"), sem("const_in")
        x_in = [sem(f"x_in{i}") for i in range(NBLK + 2)]
        ident_ready = sem("ident_ready")
        vec_t, vec_ready = sem("vec_t"), sem("vec_ready")
        taps_t = sem("taps_t")
        rows_t, rows_ready, table_in = sem("rows_t"), sem("rows_ready"), sem("table_in")
        sumsq, ms_ready, root = sem("sumsq"), sem("ms_ready"), sem("root")
        xn_ready = sem("xn_ready")
        t_ready, t_evac = sem("t_ready"), sem("t_evac")
        values_done = sem("values_done")
        t_hi = sem("t_hi")
        k_hi, v_hi_s = sem("k_hi"), sem("v_hi_s")
        s_ready, s_free = sem("s_ready"), sem("s_free")
        g_ready = sem("g_ready")
        scores_seen = sem("scores_seen")
        q_hi, q_cleared = sem("q_hi"), sem("q_cleared")
        negmax_ready, exp_done = sem("negmax_ready"), sem("exp_done")
        sinkarg_ready, sinkexp_done = sem("sinkarg_ready"), sem("sinkexp_done")
        inv_ready, pn_act = sem("inv_ready"), sem("pn_act")
        pn_ready = sem("pn_ready")
        th_done = sem("th_done")
        o_free = sem("o_free")
        c_tile = sem("c_tile")
        scratch = sem("scratch")
        bias_in = sem("bias_in")
        mk_hi_s = sem("mk_hi_s")
        lnsum_ready, centered, squared, sq_ready = sem("lnsum_ready"), sem("centered"), sem("squared"), sem("sq_ready")
        var_ready, ln_root, diag_ready = sem("var_ready"), sem("ln_root"), sem("diag_ready")
        mean_mat_ready = sem("mean_mat_ready")
        c_silu = sem("c_silu")
        o_in = [sem(f"o_in{i}") for i in range(RAW_SLOTS)]
        norm_ready = sem("norm_ready")
        oT_hi_done, oT_ready = sem("oT_hi_done"), sem("oT_ready")
        gate_done = [sem("gate_done0"), sem("gate_done1")]
        merged = sem("merged")
        y_hi, y_ready = sem("y_hi"), sem("y_ready")
        fg_in = sem("fg_in")
        out_ready, x2_in = sem("out_ready"), [sem("x2_in0"), sem("x2_in1")]
        resid, out_ss, out_ms, out_root, out_row = sem("resid"), sem("out_ss"), sem("out_ms"), sem("out_root"), sem("out_row")
        stored = [sem("stored0"), sem("stored1")]
        dve_step = sem("dve_step")

        def f32(ap):
            return ap.bitcast(F32)

        block = ctx.enter_context(nc.Block())

        @block.sync
        def _(sp):
            def load_raw(w, p, src):
                if not (isinstance(w, int) and w < 2):
                    sp.wait_ge(lo_done, w - 1)
                dst = raw[:, p, :] if len(src.shape) == 2 else raw[:, p, :].rearrange("p (k n) -> p k n", n=P)
                sp.dma_start(dst, src).then_inc(raw_in[p], 16)

            def cols(t):
                return w_in_v[:, :, ds(t * P, P)]

            for row, src in ((V_NORM, norm_g), (V_MEMNORM, mem_norm_g), (V_CONVB, conv_b),
                             (V_LNG, conv_ln_g), (V_LNB, conv_ln_b)):
                sp.dma_start(vec_nat[row:row + KD, :], src[0].rearrange("(k p) -> k p", p=P)).then_inc(vec_in, 16)
            for s in range(NBLK):
                sp.dma_start(x_nat[:, s, :], x_v[s]).then_inc(x_in[s], 16)
                if s == 3:
                    load_raw(W_K, 0, cols(COL_K))
            load_raw(W_V, 1, cols(COL_V))
            for c in range(2):
                sp.dma_start(mem_nat[:, c, :], mem[0, c * P:(c + 1) * P, :]).then_inc(x_in[NBLK + c], 16)
            sp.wait_ge(rows_ready, 2)
            sp.dma_start(bias_rows, rows_sb[:, :]).then_inc(scratch, 16)
            sp.wait_ge(scratch, 16)
            toeplitz = bass.AP(bias_rows.tensor, P - 1, [[ROW, HEADS], [-1, P], [1, 2 * P]])
            sp.dma_start(bias_table, toeplitz).then_inc(table_in, 16)
            with sp.Fori(0, KD) as t:
                load_raw(W_AB + 2 * t, 0, cols(COL_A + t))
                load_raw(W_AB + 2 * t + 1, 1, cols(COL_B + t))

            def load_bias(t):
                sp.dma_start(bias[:, :, :], bias_table[ds(2 * t, 2), :, :].rearrange("h q j -> q h j")).then_inc(bias_in, 16)

            def store_a(t):
                sp.wait_ge(o_free, 2 + 4 * t + 4)
                sp.dma_start(o_scratch[ds(t, 1), :, :].rearrange("a p s -> p (a s)"), sz_a[:, :]).then_inc(scratch, 16)

            load_raw(W_Q0, 0, cols(COL_Q))
            load_raw(W_ZQ, 1, cols(COL_ZA))
            load_raw(W_ZQ + 1, 0, cols(COL_Q + 1))
            sp.wait_ge(table_in, 16)
            sp.wait_ge(t_ready, 2 * KD + KD // 2)
            load_bias(0)

            def pair(t, next_q):
                load_raw(W_ZQ + 2 * t, 1, cols(COL_ZA + t))
                load_raw(W_ZQ + 2 * t + 1, 0, next_q)
                sp.wait_ge(s_free, S_A + 8 * t)
                load_bias(t)
                store_a(t - 1)

            with sp.Fori(1, PAIRS - 1) as t:
                pair(t, cols(COL_Q + 1 + t))
            pair(PAIRS - 1, cols(COL_QM))
            load_raw(W_M0 + 1, 1, cols(COL_QM + 1))

            def mem_tiles(w, h, store):
                for i in range(2):
                    load_raw(w + i, i, w_mem_v[:, :, ds((2 * h + i) * P, P)])
                load_raw(w + 2, 0, w_mem_v[:, :, ds(D + 2 * h * P, P)])
                store()
                load_raw(w + 3, 1, w_mem_v[:, :, ds(D + (2 * h + 1) * P, P)])

            def store_m(h):
                sp.wait_ge(o_free, 2 + O_M + 4 * h + 4)
                sp.dma_start(o_scratch[ds(KD + 2 * h, 2), :, :].rearrange("a p s -> p a s"),
                             sz_m[:, :, :]).then_inc(scratch, 16)

            mem_tiles(W_M0 + 2, 0, lambda: store_a(PAIRS - 1))
            with sp.Fori(0, MEM_HEADS - 1) as h:
                for i in range(2):
                    load_raw(W_MLOOP + 8 * h + i, i, cols(COL_ZM + 2 * h + i))
                for i in range(2):
                    load_raw(W_MLOOP + 8 * h + 2 + i, i, cols(COL_QM + 2 * (h + 1) + i))
                mem_tiles(W_MLOOP + 8 * h + 4, h + 1, lambda: store_m(h))
            for i in range(2):
                load_raw(W_MLAST + i, i, cols(COL_ZM + 2 * (MEM_HEADS - 1) + i))
            for t in range(KD):
                load_raw(W_ZC + t, t % 2, cols(COL_ZC + t))
                if t == 4:
                    store_m(MEM_HEADS - 1)

            def load_o(tiles):
                for i in tiles:
                    sp.wait_ge(oT_ready, KD if i < RAW_SLOTS else KD + i - RAW_SLOTS + 1)
                    row = (0, KD)[i // KD] + i % KD
                    sp.dma_start(o_raw[:, i % RAW_SLOTS, :], o_scratch[row]).then_inc(o_in[i % RAW_SLOTS], 16)

            def load_merge(n, e):
                br = BRANCH_ORDER[n]
                load_raw(W_MERGE + 16 * n + 2 * e, 0, cols(COL_G + KD * br + e))
                load_raw(W_MERGE + 16 * n + 2 * e + 1, 1, w_br_v[br, :, :, ds(e * P, P)])

            for n in range(3):
                load_merge(n, 0)
                if n > 0:
                    load_o(range(KD * (n - 1) + RAW_SLOTS, KD * n))
                load_merge(n, 1)
                if n == 0:
                    sp.wait_ge(scratch, 16 * (1 + PAIRS + MEM_HEADS))
                    load_o(range(RAW_SLOTS))
                elif n == 1:
                    load_o(range(KD, KD + RAW_SLOTS))
                with sp.Fori(2, KD) as e:
                    load_merge(n, e)
            for k in range(KD):
                load_raw(W_OUT + k, k % 2, w_out_v[k])
            for s in range(NBLK):
                sp.wait_ge(lo_done, W_OUT + KD)
                if s >= 2:
                    sp.wait_ge(resid, s - 1)
                sp.dma_start(raw[:, s % 2, :], x_v[s]).then_inc(x2_in[s % 2], 16)

        @block.gpsimd
        def _(pool):
            pool.sem_inc(values_done, 2)
            pool.sem_inc(o_free, 2)
            pool.sem_inc(g_ready, 2)
            pool.dma_start(conv_nat[:, :], conv_w[0]).then_inc(const_in, 16)
            pool.dma_start(rel_sb[:, :], rel_bias).then_inc(const_in, 16)
            pool.dma_start(onehot_sb[:, :], bucket_onehot).then_inc(const_in, 16)
            pool.dma_start(sink_bc[:, :], sinks[0].partition_broadcast(P)).then_inc(const_in, 16)
            nc.gpsimd.memset(mean_mat[:, :], 1.0 / D).then_inc(mean_mat_ready, 1)
            nc.gpsimd.memset(ident[:, :], 0.0).then_inc(ident_ready, 1)
            pool.wait_ge(ident_ready, 1)
            nc.gpsimd.affine_select(out=ident[:, :], in_=ident[:, :], compare_op=ALU.not_equal, fill=1.0,
                                    base=0, pattern=[[-1, P]], channel_multiplier=1).then_inc(ident_ready, 1)

            def lo_part(w, p):
                pool.wait_ge(hi_done, w + 1)
                nc.gpsimd.tensor_tensor(w_lo[:, p, :, :].rearrange("p k n -> p (k n)"), raw[:, p, :],
                                        f32(w_hi[:, p, :, :]).rearrange("p k n -> p (k n)"),
                                        ALU.subtract).then_inc(lo_done, 1)

            with pool.Fori(0, W_OUT // 2) as j:
                for p in range(2):
                    lo_part(2 * j + p, p)
            for k in range(KD):
                pool.wait_ge(hi_done, W_OUT + k + 1)
                nc.gpsimd.tensor_tensor(hT_lo[:, k, :], raw[:, k % 2, :], f32(hT_hi[:, k, :]), ALU.subtract).then_inc(lo_done, 1)
            pool.wait_ge(merged, 2 * 2 * KD)
            pool.dma_start(gate, final_norm_g.partition_broadcast(P)).then_inc(fg_in, 16)
            for s in range(NBLK):
                pool.wait_ge(out_row, s + 1)
                pool.dma_start(out_v[s], o_raw[:, s % 2, :]).then_inc(stored[s % 2], 16)
            for p in range(2):
                pool.wait_ge(stored[p], 16 * (NBLK // 2))

        @block.tensor
        def _(pe):
            mm = nc.tensor.matmul

            def split_product(dst, w_hl, x_hl, start=True, stop=True, **kw):
                mm(dst, w_hl[0], x_hl[0], start=start, stop=False, **kw)
                mm(dst, w_hl[0], x_hl[1], start=False, stop=False, **kw)
                return mm(dst, w_hl[1], x_hl[0], start=False, stop=stop, **kw)

            def project(w, p, use, src=(hT_hi, hT_lo), side=None, released=proj_free,
                        rows_ready=None):
                i = 0
                for half in range(2):
                    col = slice(half * HALF, (half + 1) * HALF)
                    dst = ps_proj[:, half, :]
                    if not (isinstance(use, int) and use == 0):
                        pe.wait_ge(released[half], use)
                    if half == 0:
                        pe.wait_ge(hi_done, w + 1)
                    for k in range(KD):
                        if rows_ready is not None and half == 0:
                            pe.wait_ge(oT_ready, rows_ready + k + 1)
                        for part in range(2):
                            mm(dst, w_hi[:, p, k, :], src[part][:, k, col], start=(k == 0 and part == 0), stop=False)
                            if side:
                                side(i)
                            i += 1
                    if half == 0:
                        pe.wait_ge(lo_done, w + 1)
                    for k in range(KD):
                        last = mm(dst, w_lo[:, p, k, :], src[0][:, k, col], start=False, stop=(k == KD - 1))
                        if k == KD - 1:
                            last.then_inc(tile_done if half else half_done, 1)
                        if side:
                            side(i)
                        i += 1

            def project_mem(w, i, use):
                dst = ps_proj[:, i, 0:MEM]
                pe.wait_ge(proj_free[i], use)
                pe.wait_ge(hi_done, w + 1)
                for k in range(KD):
                    mm(dst, w_hi[:, i, k, :], mT_hi[:, k, :], start=(k == 0), stop=False)
                    mm(dst, w_hi[:, i, k, :], mT_lo[:, k, :], start=False, stop=False)
                pe.wait_ge(lo_done, w + 1)
                for k in range(KD):
                    last = mm(dst, w_lo[:, i, k, :], mT_hi[:, k, :], start=False, stop=(k == KD - 1))
                last.then_inc(tile_done, 1)

            def turn(dst, src, n=P):
                return nc.tensor.transpose(dst, src, ident[0:n, 0:n])

            def turn_x(n):
                half, k = n // KD, n % KD
                if k == 0:
                    pe.wait_ge(xn_ready, 4 * half + 4)
                if n >= 2:
                    pe.wait_ge(t_evac, n - 1)
                for s in range(4):
                    last = turn(ps_t[:, n % 2, s * P:(s + 1) * P], x_nat[:, 4 * half + s, k * P:(k + 1) * P])
                last.then_inc(t_ready, 1)

            def turn_mem(n):
                if n == 0:
                    pe.wait_ge(xn_ready, NBLK + 2)
                pe.wait_ge(t_evac, T_MEMX + n - 1)
                for kk in range(2):
                    for c in range(2):
                        last = turn(ps_t[:, n % 2, kk * MEM + c * P:kk * MEM + (c + 1) * P],
                                    mem_nat[:, c, (2 * n + kk) * P:(2 * n + kk + 1) * P])
                last.then_inc(t_ready, 1)

            def side_x(i):
                if i in range(6, 22, 2):
                    turn_x(KD + (i - 6) // 2)
                if i == 23:
                    pe.wait_ge(t_evac, 2 * KD)

            def side_mem(i):
                if i in range(6, 46, 10):
                    turn_mem((i - 6) // 10)

            pe.wait_ge(vec_in, 16 * 5)
            pe.wait_ge(ident_ready, 2)
            turn(ps_s[:, 0, 0:NVEC], vec_nat[:, :], NVEC).then_inc(vec_t, 1)
            for n in range(KD):
                turn_x(n)
            pe.wait_ge(const_in, 16 * 4)
            for k in range(KD):
                last = turn(ps_s[:, 1, k * 32:k * 32 + TAPS], conv_nat[:, k * P:(k + 1) * P], TAPS)
            last.then_inc(taps_t, 1)
            mm(ps_o[0:HEADS, 0, 0:P], rel_sb[:, :], onehot_sb[:, :], start=True, stop=True).then_inc(rows_t, 1)
            pe.wait_ge(t_evac, KD)
            project(W_K, 0, 0, side=side_x)
            project(W_V, 1, 1, side=side_mem)
            pe.wait_ge(proj_free[1], 2)
            pe.wait_ge(vec_ready, 2)
            for c in range(2):
                for s in range(4):
                    b = 4 * c + s
                    last = turn(ps_s[:, c, s * P:(s + 1) * P], sz_a[:, b * P:(b + 1) * P])
                last.then_inc(s_ready, 1)

            with pe.Fori(0, KD) as t:
                project(W_AB + 2 * t, 0, W_AB + 2 * t)
                project(W_AB + 2 * t + 1, 1, W_AB + 2 * t + 1)

            project(W_Q0, 0, W_Q0)

            def scores(t, b):
                n = S_A + 8 * t + b
                if b == 0:
                    for half in range(2):
                        pe.wait_ge(proj_free[half], W_ZQ + 2 * t)
                pe.wait_ge(s_free, n - 1)
                q = slice(b * P, (b + 1) * P)
                lo_key = max(b - 1, 0) * P
                width = (b + 1) * P - lo_key
                for j in range(2):
                    last = split_product(ps_s[:, b % 2, j * 2 * P + 2 * P - width:(j + 1) * 2 * P],
                                         (qz_hi[:, j, q], qz_lo[:, j, q]),
                                         (kT_hi[:, lo_key:lo_key + width], kT_lo[:, lo_key:lo_key + width]))
                last.then_inc(s_ready, 1)

            def turn_probs(t, b):
                n = T_A + 8 * t + b
                if b < NORMS_ACT:
                    pe.wait_ge(pn_act, NORMS_ACT * t + b + 1)
                else:
                    pe.wait_ge(pn_ready, (NBLK - NORMS_ACT) * t + b - NORMS_ACT + 1)
                pe.wait_ge(t_evac, n - 1)
                for part in range(1 if b == 0 else 0, 2):
                    for j in range(2):
                        last = turn(ps_t[:, b % 2, (2 * part + j) * P:(2 * part + j + 1) * P],
                                    prob[:, b, j, part * P:(part + 1) * P])
                last.then_inc(t_ready, 1)

            def values(t, b):
                c = b // 2
                pe.wait_ge(t_evac, T_A + 8 * t + b + 1)
                if b % 2 == 0:
                    pe.wait_ge(o_free, 4 * t + c + 1)
                dst = ps_o[:, c % 2, (b % 2) * 2 * P:(b % 2 + 1) * 2 * P]
                for part in range(1 if b == 0 else 0, 2):
                    key = b - 1 + part
                    cols = slice(part * 2 * P, (part + 1) * 2 * P)
                    last = split_product(dst, (v_hi[:, key, :], v_lo[:, key, :]),
                                         (pt_hi[:, b % 2, cols], pt_lo[:, b % 2, cols]),
                                         start=(part == 0 or b == 0), stop=(part == 1))
                last.then_inc(values_done, 1)

            def pair(t):
                def side_scores(i):
                    if i >= 8 and (i - 8) % 5 == 0:
                        scores(t, (i - 8) // 5)

                def side_values(i):
                    for b in range(NBLK):
                        if i == 5 + 5 * b:
                            turn_probs(t, b)
                        if i == min(13 + 5 * b, 47):
                            values(t, b)

                project(W_ZQ + 2 * t, 1, W_ZQ + 2 * t, side=side_scores)
                project(W_ZQ + 2 * t + 1, 0, W_ZQ + 2 * t + 1, side=side_values)

            with pe.Fori(0, PAIRS) as t:
                pair(t)

            def mem_kv(w, use, t_use):
                for i in range(2):
                    project_mem(w + i, i, use)
                for i in range(2):
                    project_mem(w + 2 + i, i, use + 1)
                for i in range(2):
                    pe.wait_ge(proj_free[i], use + 2)
                pe.wait_ge(t_evac, t_use)
                for c in range(2):
                    for i in range(2):
                        last = turn(ps_t[:, 0, c * MEM + i * P:c * MEM + (i + 1) * P], mvT[:, i, c * P:(c + 1) * P])
                last.then_inc(t_ready, 1)

            def mem_scores(h, b):
                if b == 0:
                    for i in range(2):
                        pe.wait_ge(proj_free[i], U_MLOOP + 6 * h)
                pe.wait_ge(exp_done, 8 * PAIRS + 8 * h + b - 1)
                q = slice(b * P, (b + 1) * P)
                for i in range(2):
                    last = split_product(ps_s[:, b % 2, 0:MEM], (qm_hi[:, i, q], qm_lo[:, i, q]),
                                         (mk_hi[:, i, :], mk_lo[:, i, :]), start=(i == 0), stop=(i == 1))
                last.then_inc(s_ready, 1)

            def mem_turn(h, c, t_use, bank):
                pe.wait_ge(pn_act, NORMS_ACT * PAIRS + 4 * h + c + 1)
                pe.wait_ge(t_evac, t_use - 1)
                for part in range(2):
                    for i in range(2):
                        last = turn(ps_t[:, bank, part * MEM + i * P:part * MEM + (i + 1) * P],
                                    prob_m[:, 2 * c + i, part * P:(part + 1) * P])
                last.then_inc(t_ready, 1)

            def mem_values(h, c, t_use):
                pe.wait_ge(t_evac, t_use + 1)
                pe.wait_ge(o_free, O_M + 4 * h + c + 1)
                for i in range(2):
                    dst = ps_o[:, c % 2, i * MEM:(i + 1) * MEM]
                    for part in range(2):
                        last = split_product(dst, (mv_hi[:, part, i * P:(i + 1) * P], mv_lo[:, part, i * P:(i + 1) * P]),
                                             (ptm_hi[:, c % 2, part * MEM:(part + 1) * MEM],
                                              ptm_lo[:, c % 2, part * MEM:(part + 1) * MEM]),
                                             start=(part == 0), stop=(part == 1))
                last.then_inc(values_done, 1)

            def channel_means():
                pe.wait_ge(mean_mat_ready, 1)
                pe.wait_ge(exp_done, 8 * (PAIRS + MEM_HEADS))
                pe.wait_ge(lnsum_ready, 1)
                for half in range(2):
                    mm(ps_s[:, half, :], mean_mat[:, :], ln_sum[:, half * HALF:(half + 1) * HALF],
                       start=True, stop=True).then_inc(s_ready, 1)

            def channel_variances():
                pe.wait_ge(lnsum_ready, 2)
                for b in range(NBLK):
                    last = mm(ps_t[:, 0, b:b + 1], ln_sum[:, b * P:(b + 1) * P], mean_mat[:, 0:1], start=True, stop=True)
                last.then_inc(s_ready, 1)

            def spread_rstd():
                pe.wait_ge(diag_ready, 1)
                for half in range(2):
                    mm(ps_s[:, half, :], mean_mat[:, :],
                       rstd_diag[:, 4 * half:4 * half + 4, :].rearrange("p b q -> p (b q)"),
                       start=True, stop=True).then_inc(s_ready, 1)

            def mem_head(h, w, use, t_use, last_head):
                def side_scores(first):
                    def side(i):
                        if i % 12 == 5:
                            mem_scores(h, first + i // 12)
                    return side

                def side_values(first):
                    def side(i):
                        if i == 2 and first == 0 and last_head:
                            channel_means()
                        for c in range(2):
                            if i == 4 + 20 * c:
                                mem_turn(h, first + c, t_use + first + c, 1 - (first + c) % 2)
                            if i == 16 + 20 * c:
                                mem_values(h, first + c, t_use + first + c)
                    return side

                project(w, 0, use, side=side_scores(0))
                project(w + 1, 1, use + 1, side=side_scores(4))
                project(w + 2, 0, use + 2, side=side_values(0))
                project(w + 3, 1, use + 3, side=side_values(2))
                if not last_head:
                    mem_kv(w + 4, use + 4, t_use + 4)

            project(W_M0 + 1, 1, U_M0 + 1)
            mem_kv(W_M0 + 2, U_M0 + 2, T_MV0)
            with pe.Fori(0, MEM_HEADS - 1) as h:
                mem_head(h, W_MLOOP + 8 * h, U_MLOOP + 6 * h, T_MLOOP + 5 * h, False)
            mem_head(MEM_HEADS - 1, W_MLAST, U_MLAST, T_MLOOP + 5 * (MEM_HEADS - 1), True)

            for t in range(2, KD):
                if t == 3:
                    channel_variances()

                def side(i):
                    if t == 3 and i == 16:
                        spread_rstd()
                project(W_ZC + t, t % 2, U_ZC + t, side=side)

            def merge_step(n, e, by_k):
                w = W_MERGE + 16 * n + 2 * e
                project(w, 0, U_MERGE + 8 * n + e)
                project(w + 1, 1, 8 * n + e + 1, src=(oT_hi, oT_lo), released=gate_done,
                        rows_ready=KD * n if by_k else None)

            for n in range(3):
                merge_step(n, 0, True)
                with pe.Fori(1, KD) as e:
                    merge_step(n, e, False)

            out_banks = [ps_s, ps_t, ps_o, ps_proj]

            def out_pass(s, k):
                rows = slice(s * P, (s + 1) * P)
                for half in range(2):
                    cols = slice(half * HALF, (half + 1) * HALF)
                    last = split_product(out_banks[s % 4][:, half, :], (oT_hi[:, k, rows], oT_lo[:, k, rows]),
                                         (hT_hi[:, k, cols], hT_lo[:, k, cols]), start=(k == 0), stop=(k == KD - 1))
                return last

            for k in range(KD):
                pe.wait_ge(y_ready, k + 1)
                pe.wait_ge(lo_done, W_OUT + k + 1)
                for s in range(4):
                    if k == 0 and s == 3:
                        pe.wait_ge(merged, 2 * 2 * KD)
                    last = out_pass(s, k)
                    if k == KD - 1:
                        last.then_inc(out_ready, 1)
            for s in range(4, NBLK):
                pe.wait_ge(resid, s - 3)
                for k in range(KD):
                    last = out_pass(s, k)
                last.then_inc(out_ready, 1)

        @block.scalar
        def _(act):
            def copy_hi(dst, src, scale=1.0):
                return nc.scalar.activation(dst, src, ACT.Copy, scale=scale)

            def hi_part(w, p, n):
                act.wait_ge(raw_in[p], 16 * (n + 1))
                if not (isinstance(w, int) and w < 2):
                    act.wait_ge(tile_done, w - 1)
                copy_hi(w_hi[:, p, :, :].rearrange("p k n -> p (k n)"), raw[:, p, :]).then_inc(hi_done, 1)

            def wait_half(half, w, full):
                if half == 0:
                    act.wait_ge(half_done, full + 1)
                else:
                    act.wait_ge(tile_done, w + 1)

            def half_cols(half):
                return slice(half * HALF, (half + 1) * HALF)

            def squares(rows):
                for s in rows:
                    src = x_nat[:, s, :] if s < NBLK else mem_nat[:, s - NBLK, :]
                    act.wait_ge(x_in[s], 16)
                    nc.scalar.activation(unused_squares[:, :], src, ACT.Square,
                                         accum_out=sums[:, s:s + 1]).then_inc(sumsq, 1)
                    act.wait_ge(sumsq, s + 1)

            def roots(grp):
                rows = NORM_GROUPS[grp]
                act.wait_ge(ms_ready, grp + 1)
                ms = sums[:, MS + rows[0]:MS + rows[-1] + 1]
                nc.scalar.activation(ms, ms, ACT.Sqrt).then_inc(root, 1)

            def x_hi(n):
                half, k = n // KD, n % KD
                act.wait_ge(t_ready, n + 1)
                copy_hi(hT_hi[:, k, half_cols(half)], ps_t[:, n % 2, :],
                        vec[:, V_NORM + k:V_NORM + k + 1]).then_inc(t_hi, 1)

            def k_hi_half(half):
                wait_half(half, W_K, W_K)
                copy_hi(kT_hi[:, half_cols(half)], ps_proj[:, half, :]).then_inc(k_hi, 1)

            squares(NORM_GROUPS[0])
            roots(0)
            squares(range(4, 6))
            act.wait_ge(vec_ready, 1)
            x_hi(0)
            x_hi(1)
            for n in range(2, 4):
                squares(range(n + 4, n + 5))
                x_hi(n)
            roots(1)
            for n in range(4, KD):
                x_hi(n)
                if n == 5:
                    hi_part(W_K, 0, 0)
            hi_part(W_V, 1, 0)
            for n in range(KD, 2 * KD):
                x_hi(n)
            squares(NORM_GROUPS[2])
            roots(2)
            for n in range(KD // 2):
                if n % 2 == 0:
                    k_hi_half(n // 2)
                act.wait_ge(t_ready, T_MEMX + n + 1)
                for kk in range(2):
                    k = 2 * n + kk
                    last = copy_hi(mT_hi[:, k, :], ps_t[:, n % 2, kk * MEM:(kk + 1) * MEM],
                                   vec[:, V_MEMNORM + k:V_MEMNORM + k + 1])
                last.then_inc(t_hi, 1)
            hi_part(W_AB, 0, 1)
            for half in range(2):
                wait_half(half, W_V, W_V)
                copy_hi(sz_a[:, half_cols(half)], ps_proj[:, half, :]).then_inc(proj_free[half], 1)
            for c in range(2):
                act.wait_ge(s_ready, c + 1)
                copy_hi(v_hi[:, 4 * c:4 * c + 4, :].rearrange("p b n -> p (b n)"), ps_s[:, c, :]).then_inc(v_hi_s, 1)

            with act.Fori(0, KD) as t:
                hi_part(W_AB + 2 * t + 1, 1, 1 + t)
                for half in range(2):
                    wait_half(half, W_AB + 2 * t, W_AB + 2 * t)
                    copy_hi(conv[:, ds(t + 1, 1), PAD + half * HALF:PAD + (half + 1) * HALF]
                            .rearrange("p a s -> p (a s)"), ps_proj[:, half, :]).then_inc(proj_free[half], 1)
                hi_part(W_AB + 2 * t + 2, 0, 2 + t)
                for half in range(2):
                    wait_half(half, W_AB + 2 * t + 1, W_AB + 2 * t + 1)
                    act.wait_ge(g_ready, 2 * t + half + 1)
                    nc.scalar.activation(th_a[:, half, :], ps_proj[:, half, :], ACT.Sigmoid).then_inc(proj_free[half], 1)

            def q_hi_part(half, w, g):
                wait_half(half, w, w)
                for j in range(2):
                    last = copy_hi(qz_hi[64 * g:64 * g + 64, j, half_cols(half)],
                                   ps_proj[64 * j:64 * j + 64, half, :], HEAD_DIM ** -0.5)
                last.then_inc(q_hi, 1)

            hi_part(W_ZQ, 1, W_ZQ // 2)
            act.wait_ge(q_cleared, 2)
            for half in range(2):
                q_hi_part(half, W_Q0, 0)

            def qm_hi_part(i, half, w, full):
                wait_half(half, w, full)
                copy_hi(qm_hi[:, i, half_cols(half)], ps_proj[:, half, :], MEM ** -0.5).then_inc(q_hi, 1)

            def pair(g_next, t):
                w = W_ZQ + 2 * t

                def next_q(half):
                    if g_next is None:
                        qm_hi_part(0, half, w + 1, w + 1)
                    else:
                        q_hi_part(half, w + 1, g_next)

                def block_exp(b):
                    act.wait_ge(negmax_ready, 8 * t + b + 1)
                    first = P if b == 0 else 0
                    for j in range(2):
                        seg = prob[:, b, j, first:]
                        last = nc.scalar.activation(seg, seg, ACT.Exp, bias=neg_max[:, b, j:j + 1],
                                                    accum_out=row_sum[:, b, j:j + 1])
                    last.then_inc(exp_done, 1)

                def tanh_half(half):
                    wait_half(half, w, w)
                    act.wait_ge(scratch, 16 * (1 + t))
                    nc.scalar.activation(th_a[:, half, :], ps_proj[:, half, :], ACT.Tanh, scale=0.5).then_inc(th_done, 1)

                def sink(grp):
                    act.wait_ge(sinkarg_ready, 2 * t + grp + 1)
                    nc.scalar.activation(sink_exp[:, 4 * grp:4 * grp + 4, :], sink_arg[:, 4 * grp:4 * grp + 4, :],
                                         ACT.Exp).then_inc(sinkexp_done, 1)

                def norm(b):
                    first = P if b == 0 else 0
                    if b == 0:
                        act.wait_ge(inv_ready, t + 1)
                    for j in range(2):
                        last = copy_hi(prob[:, b, j, first:], prob[:, b, j, first:], inv_sum[:, b, j:j + 1])
                    last.then_inc(pn_act, 1)

                hi_part(w + 1, 0, W_ZQ // 2 + 1 + t)
                for b in range(NBLK):
                    block_exp(b)
                    if b == 6:
                        norm(0)
                    if b == 3:
                        sink(0)
                    if b == 4:
                        tanh_half(0)
                tanh_half(1)
                norm(1)
                sink(1)
                for b in range(NBLK):
                    n = 8 * t + b
                    if b == 2:
                        hi_part(w + 2, 1, W_ZQ // 2 + 1 + t)
                    act.wait_ge(t_ready, T_A + n + 1)
                    act.wait_ge(values_done, n + 1)
                    first = 2 * P if b == 0 else 0
                    copy_hi(pt_hi[:, b % 2, first:], ps_t[:, b % 2, first:]).then_inc(t_hi, 1)
                    if b + 2 < NORMS_ACT:
                        norm(b + 2)
                    if b == 4:
                        if g_next == 1 and isinstance(t, int):
                            act.wait_ge(q_cleared, 6)
                        next_q(0)
                next_q(1)

            for g in range(KV_HEADS):
                with act.Fori(0, PAIRS_PER_KV - 1) as t4:
                    pair(g, PAIRS_PER_KV * g + t4)
                pair((1, None)[g], PAIRS_PER_KV * g + PAIRS_PER_KV - 1)

            def mem_kv(w, n, t_use):
                for i in range(2):
                    hi_part(w + 1 + i, 1 - i, n + i)
                    act.wait_ge(tile_done, w + i + 1)
                    copy_hi(mk_hi[:, i, :], ps_proj[:, i, 0:MEM]).then_inc(mk_hi_s, 1)
                for i in range(2):
                    hi_part(w + 3 + i, 1 - i, n + 1 + i)
                    act.wait_ge(tile_done, w + 2 + i + 1)
                    copy_hi(mvT[:, i, :], ps_proj[:, i, 0:MEM]).then_inc(proj_free[i], 1)
                act.wait_ge(t_ready, t_use + 1)
                copy_hi(mv_hi[:, :, :].rearrange("p c n -> p (c n)"), ps_t[:, 0, :]).then_inc(t_hi, 1)

            def mem_head(h, w, full, t_use, n, last_head):
                def block_exp(b):
                    act.wait_ge(negmax_ready, 8 * PAIRS + 8 * h + b + 1)
                    nc.scalar.activation(prob_m[:, b, :], ps_s[:, b % 2, 0:MEM], ACT.Exp, bias=neg_max[:, b, 0:1],
                                         accum_out=row_sum[:, b, 0:1]).then_inc(exp_done, 1)

                def tanh_half(i, half):
                    wait_half(half, w + i, full + i)
                    nc.scalar.activation(th_m[:, half, :], ps_proj[:, half, :], ACT.Tanh, scale=0.5).then_inc(th_done, 1)

                def norm(c):
                    if c % 2 == 0:
                        act.wait_ge(inv_ready, PAIRS + 2 * h + c // 2 + 1)
                    for b in (2 * c, 2 * c + 1):
                        last = copy_hi(prob_m[:, b, :], prob_m[:, b, :], inv_sum[:, b, 0:1])
                    last.then_inc(pn_act, 1)

                for i in range(2):
                    hi_part(w + 1 + i, 1 - i, n + i)
                    for b in range(4):
                        block_exp(4 * i + b)
                        if b == 2:
                            tanh_half(i, 0)
                        if i == 1 and b == 2:
                            norm(0)
                    tanh_half(i, 1)
                for i in range(2):
                    for c in (2 * i, 2 * i + 1):
                        act.wait_ge(t_ready, t_use + c + 1)
                        act.wait_ge(values_done, PT_M + 4 * h + c + 1)
                        copy_hi(ptm_hi[:, c % 2, :], ps_t[:, 1 - c % 2, :]).then_inc(t_hi, 1)
                        if c < 3:
                            norm(c + 1)
                        if c == 2 * i:
                            hi_part(w + 3 + i, 1 - i, n + 1 + i)
                        if last_head and c > 0:
                            square(2 * c - 2)
                            square(2 * c - 1)
                    for half in range(2):
                        if last_head:
                            silu_zc(i, half)
                        else:
                            qm_hi_part(i, half, w + 2 + i, full + 2 + i)
                if not last_head:
                    mem_kv(w + 4, n + 2, t_use + 4)

            def square(t):
                act.wait_ge(centered, t + 1)
                if t >= 2:
                    act.wait_ge(squared, t - 1)
                nc.scalar.activation(ln_sq[:, t % 2, :], conv[:, t, PAD:], ACT.Square).then_inc(sq_ready, 1)

            def silu_zc(t, half):
                wait_half(half, W_ZC + t, F_ZC + t)
                if t >= ZC_SLOTS:
                    act.wait_ge(c_tile, t - ZC_SLOTS + 1)
                nc.scalar.activation(sz_c[:, t % ZC_SLOTS, half_cols(half)], ps_proj[:, half, :],
                                     ACT.Silu).then_inc(proj_free[half], 1)

            hi_part(W_M0 + 2, 0, W_M0 // 2 + 1)
            for half in range(2):
                qm_hi_part(1, half, W_M0 + 1, F_M0 + 1)
            mem_kv(W_M0 + 2, W_M0 // 2 + 1, T_MV0)
            with act.Fori(0, MEM_HEADS - 1) as h:
                mem_head(h, W_MLOOP + 8 * h, F_MLOOP + 4 * h, T_MLOOP + 5 * h, W_MLOOP // 2 + 4 * h, False)
            mem_head(MEM_HEADS - 1, W_MLAST, F_MLAST, T_MLOOP + 5 * (MEM_HEADS - 1), W_MLAST // 2, True)

            hi_part(W_ZC + 3, 1, W_ZC // 2 + 1)
            for t in (KD - 2, KD - 1):
                square(t)
            for half in range(2):
                silu_zc(2, half)
            hi_part(W_ZC + 4, 0, W_ZC // 2 + 2)
            act.wait_ge(var_ready, 1)
            ms = sums[:, MS:MS + NBLK]
            nc.scalar.activation(ms, ms, ACT.Sqrt).then_inc(ln_root, 1)
            def z_tile(t):
                for half in range(2):
                    silu_zc(t, half)
                if t < KD - 1:
                    hi_part(W_ZC + t + 2, t % 2, (W_ZC + t + 2) // 2)

            def silu_norm(t):
                act.wait_ge(norm_ready, t + 1)
                nc.scalar.activation(conv[:, t, PAD:], conv[:, t, PAD:], ACT.Silu, scale=vec[:, V_LNG + t:V_LNG + t + 1],
                                     bias=vec[:, V_LNB + t:V_LNB + t + 1]).then_inc(c_silu, 1)

            def c_hi(t):
                act.wait_ge(c_tile, t + 1)
                copy_hi(oT_hi[:, t, :], conv[:, t, PAD:]).then_inc(oT_hi_done, 1)

            silu_norm(0)
            silu_norm(1)
            z_tile(3)
            for t in range(2, 4):
                c_hi(t - 2)
                silu_norm(t)
            c_hi(2)
            c_hi(3)
            for t in range(4, KD):
                silu_norm(t)
                z_tile(t)
                c_hi(t)

            def merge_step(n, e, first_step, last_step):
                w, full = W_MERGE + 16 * n + 2 * e, F_MERGE + 16 * n + 2 * e

                def gate_half(half):
                    wait_half(half, w, full)
                    if n > 0 and not (n == 1 and first_step):
                        act.wait_ge(merged, 16 * (n - 1) + 2 * e + half - 1)
                    nc.scalar.activation(gate[:, half_cols(half)], ps_proj[:, half, :],
                                         ACT.Sigmoid).then_inc(gate_done[half], 1)

                def row_hi(k):
                    i = KD * (n - 1) + k
                    act.wait_ge(o_in[i % RAW_SLOTS], 16 * (i // RAW_SLOTS + 1))
                    copy_hi(oT_hi[:, k, :], o_raw[:, i % RAW_SLOTS, :]).then_inc(oT_hi_done, 1)

                hi_part(w + 1, 1, W_MERGE // 2 + 8 * n + e)
                if first_step and n > 0:
                    for k in range(KD - 3):
                        row_hi(k)
                    gate_half(0)
                    for k in range(KD - 3, KD):
                        row_hi(k)
                    gate_half(1)
                else:
                    for half in range(2):
                        gate_half(half)
                if not last_step:
                    hi_part(w + 2, 0, W_MERGE // 2 + 8 * n + e + 1)

            for n in range(3):
                merge_step(n, 0, True, False)
                with act.Fori(1, KD - 1) as e:
                    merge_step(n, e, False, False)
                merge_step(n, KD - 1, False, n == 2)

            act.wait_ge(tile_done, W_OUT)
            for k in range(KD):
                act.wait_ge(raw_in[k % 2], 16 * (W_OUT // 2 + k // 2 + 1))
                copy_hi(hT_hi[:, k, :], raw[:, k % 2, :]).then_inc(hi_done, 1)
                act.wait_ge(merged, 2 * KD + 2 * (k + 1))
                copy_hi(oT_hi[:, k, :], yT[:, k, :]).then_inc(y_hi, 1)
            act.wait_ge(y_ready, KD)
            for s in range(NBLK):
                act.wait_ge(resid, s + 1)
                nc.scalar.activation(yT[:, s, :], o_raw[:, s % 2, :], ACT.Square,
                                     accum_out=sums[:, s:s + 1]).then_inc(out_ss, 1)
                act.wait_ge(out_ms, s + 1)
                nc.scalar.activation(sums[:, MS + s:MS + s + 1], sums[:, MS + s:MS + s + 1], ACT.Sqrt).then_inc(out_root, 1)

        @block.vector
        def _(dve):
            steps = Tally(dve, dve_step)
            v = nc.vector

            def rest(dst, src, hi, scale=1.0):
                return v.scalar_tensor_tensor(out=dst, in0=src, scalar=scale, in1=f32(hi),
                                              op0=ALU.mult, op1=ALU.subtract)

            def wait_half(half, w, full):
                if half == 0:
                    dve.wait_ge(half_done, full + 1)
                else:
                    dve.wait_ge(tile_done, w + 1)

            def half_cols(half):
                return slice(half * HALF, (half + 1) * HALF)

            def flat(ap):
                return ap.rearrange("p a s -> p (a s)")

            def tap(c, k, first=False):
                y = late_tiles[:, c - 6, :] if isinstance(c, int) and c >= 6 else flat(conv[:, ds(c, 1), PAD:])
                g = flat(conv[:, ds(c + 1, 1), ds(k, S)])
                w = flat(taps[:, ds(c, 1), ds(k, 1)])
                steps.wait()
                if first:
                    steps.tick(v.tensor_scalar(y, g, w, vec[:, ds(V_CONVB + c, 1)], ALU.mult, ALU.add))
                else:
                    steps.tick(v.scalar_tensor_tensor(out=y, in0=g, scalar=w, in1=y, op0=ALU.mult, op1=ALU.add))

            for c in range(KD + 1):
                steps.tick(v.memset(conv[:, c, 0:PAD], 0.0))
            v.memset(rows_sb[:, :], MASKED).then_inc(rows_ready, 1)
            dve.wait_ge(vec_t, 1)
            v.tensor_copy(vec[:, :], ps_s[:, 0, 0:NVEC]).then_inc(vec_ready, 1)

            def inverse_roots(grp):
                rows = NORM_GROUPS[grp]
                ms = sums[:, MS + rows[0]:MS + rows[-1] + 1]
                dve.wait_ge(sumsq, rows[-1] + 1)
                v.tensor_scalar(ms, sums[:, rows[0]:rows[-1] + 1], 1.0 / D, RMS_EPS, ALU.mult, ALU.add).then_inc(ms_ready, 1)
                dve.wait_ge(root, grp + 1)
                steps.tick(v.reciprocal(ms, ms))

            def normed(grp):
                steps.wait()
                for s in NORM_GROUPS[grp]:
                    row = x_nat[:, s, :] if s < NBLK else mem_nat[:, s - NBLK, :]
                    v.tensor_scalar(row, row, sums[:, MS + s:MS + s + 1], None, ALU.mult).then_inc(xn_ready, 1)

            def x_lo(n):
                half, k = n // KD, n % KD
                dve.wait_ge(t_hi, n + 1)
                rest(hT_lo[:, k, half_cols(half)], ps_t[:, n % 2, :], hT_hi[:, k, half_cols(half)],
                     vec[:, V_NORM + k:V_NORM + k + 1]).then_inc(t_evac, 1)

            def k_lo_half(half):
                dve.wait_ge(k_hi, half + 1)
                rest(kT_lo[:, half_cols(half)], ps_proj[:, half, :], kT_hi[:, half_cols(half)]).then_inc(proj_free[half], 1)

            inverse_roots(0)
            normed(0)
            dve.wait_ge(vec_ready, 1)
            for n in range(KD):
                x_lo(n)
                if n == 3:
                    inverse_roots(1)
            normed(1)
            dve.wait_ge(taps_t, 1)
            v.tensor_copy(taps[:, :, :], ps_s[:, 1, 0:KD * 32].rearrange("p (k t) -> p k t", t=32)[:, :, 0:TAPS]).then_inc(vec_ready, 1)
            dve.wait_ge(rows_t, 1)
            dve.wait_ge(rows_ready, 1)
            v.tensor_copy(rows_sb[:, P:2 * P], ps_o[0:HEADS, 0, 0:P]).then_inc(rows_ready, 1)
            steps.tick(v.tensor_scalar(neg_sink[:, :], sink_bc[:, :], -1.0, None, ALU.mult))
            for n in range(KD, 2 * KD):
                x_lo(n)
            inverse_roots(2)
            normed(2)
            for n in range(KD // 2):
                if n % 2 == 0:
                    k_lo_half(n // 2)
                dve.wait_ge(t_hi, T_MEMX + n + 1)
                for kk in range(2):
                    k = 2 * n + kk
                    last = rest(mT_lo[:, k, :], ps_t[:, n % 2, kk * MEM:(kk + 1) * MEM], mT_hi[:, k, :],
                                vec[:, V_MEMNORM + k:V_MEMNORM + k + 1])
                    if kk == 0:
                        steps.tick(last)
                last.then_inc(t_evac, 1)
            dve.wait_ge(t_ready, 2 * KD + KD // 2)
            for part in (qz_hi, qz_lo):
                v.memset(f32(part[64:128, :, :]), 0.0).then_inc(q_cleared, 1)
            for c in range(2):
                dve.wait_ge(v_hi_s, c + 1)
                rest(v_lo[:, 4 * c:4 * c + 4, :].rearrange("p b n -> p (b n)"), ps_s[:, c, :],
                     v_hi[:, 4 * c:4 * c + 4, :].rearrange("p b n -> p (b n)")).then_inc(s_free, 1)

            def gated(t, half):
                g = flat(conv[:, ds(t + 1, 1), PAD + half * HALF:PAD + (half + 1) * HALF])
                dve.wait_ge(proj_free[half], W_AB + 2 * t + 2)
                v.tensor_tensor(g, g, th_a[:, half, :], ALU.mult).then_inc(g_ready, 1)

            todo = [(c, k) for c in range(4) for k in range(TAPS)]
            for t in range(KD):
                for half in range(2):
                    gated(t, half)
                dve.wait_ge(g_ready, 2 + 2 * t + 2)
                part = 14 if t < KD - 1 else 5
                for c, k in todo[:part]:
                    tap(c, k, k == 0)
                del todo[:part]

            def q_lo_part(half, g):
                for jj in range(2):
                    rows, src = slice(64 * g, 64 * g + 64), slice(64 * jj, 64 * jj + 64)
                    last = rest(qz_lo[rows, jj, half_cols(half)], ps_proj[src, half, :],
                                qz_hi[rows, jj, half_cols(half)], HEAD_DIM ** -0.5)
                    if jj == 0:
                        steps.tick(last)
                last.then_inc(proj_free[half], 1)

            def qm_lo_part(i, half, n):
                dve.wait_ge(q_hi, n + 1)
                rest(qm_lo[:, i, half_cols(half)], ps_proj[:, half, :], qm_hi[:, i, half_cols(half)],
                     MEM ** -0.5).then_inc(proj_free[half], 1)

            def pair(g, g_next, t, todo):
                w = W_ZQ + 2 * t

                def next_q(half):
                    if g_next is None:
                        qm_lo_part(0, half, 2 * PAIRS + half)
                    else:
                        dve.wait_ge(q_hi, 2 * t + 3 + half)
                        q_lo_part(half, g_next)

                def some(n):
                    for c, k in todo[:n]:
                        tap(c, k, k == 0 if isinstance(k, int) else False)
                    del todo[:n]

                def norm(b):
                    for j in range(2):
                        last = v.tensor_scalar(prob[:, b, j, :], prob[:, b, j, :], inv_sum[:, b, j:j + 1], None, ALU.mult)
                        if j == 0:
                            steps.tick(last)
                    last.then_inc(pn_ready, 1)

                def biased(b):
                    first = P if b == 0 else 0
                    dve.wait_ge(s_ready, S_A + 8 * t + b + 1)
                    dve.sem_inc(scores_seen, 1)
                    for j in range(2):
                        last = v.tensor_tensor_reduce(prob[:, b, j, first:], ps_s[:, b % 2, j * 2 * P + first:(j + 1) * 2 * P],
                                                      bias[:, j, first:], 1.0, MASKED, ALU.add, ALU.max, row_max[:, b, j:j + 1])
                        if j == 0:
                            steps.tick(last)
                    last.then_inc(s_free, 1)
                    steps.wait()
                    dve.wait_ge(s_free, S_A + 8 * t + b + 1)
                    v.scalar_tensor_tensor(out=neg_max[:, b, :], in0=row_max[:, b, :], scalar=-1.0,
                                           in1=neg_sink[:, ds(2 * t, 2)], op0=ALU.mult, op1=ALU.min).then_inc(negmax_ready, 1)

                def sink_args(grp):
                    blocks = slice(4 * grp, 4 * grp + 4)
                    dve.wait_ge(negmax_ready, 8 * t + 4 * grp + 4)
                    for j in range(2):
                        last = v.tensor_scalar(sink_arg[:, blocks, j], neg_max[:, blocks, j], sink_bc[:, ds(2 * t + j, 1)],
                                               None, ALU.add)
                        if j == 0:
                            steps.tick(last)
                    last.then_inc(sinkarg_ready, 1)

                def inverses(grp):
                    blocks = slice(4 * grp, 4 * grp + 4)
                    dve.wait_ge(exp_done, 8 * t + 4 * grp + 4)
                    dve.wait_ge(sinkexp_done, 2 * t + grp + 1)
                    steps.tick(v.tensor_tensor(row_sum[:, blocks, :], row_sum[:, blocks, :], sink_exp[:, blocks, :], ALU.add))
                    steps.wait()
                    steps.tick(v.reciprocal(row_sum[:, blocks, :], row_sum[:, blocks, :]))
                    steps.wait()
                    last = v.tensor_scalar(inv_sum[:, blocks, :], row_sum[:, blocks, :], 0.5, None, ALU.mult)
                    if grp == 0:
                        last.then_inc(inv_ready, 1)
                    else:
                        steps.tick(last)

                def silu_half(half):
                    dve.wait_ge(th_done, 2 * t + half + 1)
                    v.scalar_tensor_tensor(out=sz_a[:, half_cols(half)], in0=th_a[:, half, :], scalar=1.0,
                                           in1=ps_proj[:, half, :], op0=ALU.add, op1=ALU.mult).then_inc(proj_free[half], 1)

                dve.wait_ge(bias_in, 16 * (t + 1))
                dve.wait_ge(t_ready, T_A + 8 * t)
                for b in range(NBLK):
                    biased(b)
                    if b == 3:
                        sink_args(0)
                    if b in (1, 2):
                        some(1)
                    if b == 5:
                        silu_half(0)
                        inverses(0)
                sink_args(1)
                silu_half(1)
                inverses(1)
                steps.wait()
                for b in range(NBLK + 2):
                    if 2 <= b < 2 + NBLK - NORMS_ACT:
                        norm(b + NORMS_ACT - 2)
                    if 1 <= b <= NBLK:
                        c = b - 1
                        first = 2 * P if c == 0 else 0
                        dve.wait_ge(t_hi, T_A + 8 * t + c + 1)
                        rest(pt_lo[:, c % 2, first:], ps_t[:, c % 2, first:], pt_hi[:, c % 2, first:]).then_inc(t_evac, 1)
                    if b >= 3 and b % 2 == 1:
                        c = (b - 3) // 2
                        dve.wait_ge(values_done, 2 + 8 * t + 2 * c + 2)
                        if c == 0:
                            dve.wait_ge(proj_free[0], w + 1)
                            dve.wait_ge(proj_free[1], w + 1)
                        for j in range(2):
                            o = sz_a[64 * j:64 * j + 64, 2 * c * P:(2 * c + 2) * P].rearrange("p (b q) -> p b q", q=P)
                            src = ps_o[64 * g:64 * g + 64, c % 2, :].rearrange("p (b h q) -> p b h q", b=2, h=2)[:, :, j, :]
                            last = v.tensor_tensor(o, src, o, ALU.mult)
                            if j == 0:
                                steps.tick(last)
                        last.then_inc(o_free, 1)
                    if b == 5:
                        next_q(0)
                    if 1 <= b <= 4 and g_next is not None and g_next != g:
                        part, jj = (qz_hi, qz_lo)[b % 2], (b - 1) // 2
                        v.memset(f32(part[0:64, jj, :]), 0.0).then_inc(q_cleared, 1)
                    elif b in (6, 7, 8):
                        some(1)
                next_q(1)
                some(99)

            for half in range(2):
                dve.wait_ge(q_hi, half + 1)
                q_lo_part(half, 0)
            for g in range(KV_HEADS):
                per, before = 5, (10, 1)[g]
                if g == 1:
                    tap(4, 0, True)
                for t4 in steps.loop(PAIRS_PER_KV - 1, PAIR_STEPS + per):
                    pair(g, g, PAIRS_PER_KV * g + t4, [(3 + g, before + per * t4 + i) for i in range(per)])
                pair(g, (1, None)[g], PAIRS_PER_KV * g + PAIRS_PER_KV - 1,
                     [(3, k) for k in range(25, TAPS)] if g == 0 else [(4, k) for k in range(16, 21)])

            def mem_kv(w, heads_before, t_use, between):
                for i in range(2):
                    between()
                    dve.wait_ge(mk_hi_s, 2 * heads_before + i + 1)
                    rest(mk_lo[:, i, :], ps_proj[:, i, 0:MEM], mk_hi[:, i, :]).then_inc(proj_free[i], 1)
                between()
                dve.wait_ge(t_hi, t_use + 1)
                rest(flat(mv_lo[:, :, :]), ps_t[:, 0, :], flat(mv_hi[:, :, :])).then_inc(t_evac, 1)

            def mem_head(h, w, t_use, last_head, todo):
                def some(n):
                    for c, k in todo[:n]:
                        tap(c, k)
                    del todo[:n]

                def maximum(b):
                    dve.wait_ge(s_ready, S_M + 8 * h + b + 1)
                    steps.tick(v.tensor_reduce(row_max[:, b, 0:1], ps_s[:, b % 2, 0:MEM], AX.X, ALU.max))
                    steps.wait()
                    v.tensor_scalar(neg_max[:, b, 0:1], row_max[:, b, 0:1], -1.0, None, ALU.mult).then_inc(negmax_ready, 1)

                def silu_half(i, half):
                    dve.wait_ge(th_done, 2 * PAIRS + 4 * h + 2 * i + half + 1)
                    dve.wait_ge(scratch, 16 * (1 + PAIRS + h))
                    v.scalar_tensor_tensor(out=sz_m[:, i, half_cols(half)], in0=th_m[:, half, :], scalar=1.0,
                                           in1=ps_proj[:, half, :], op0=ALU.add, op1=ALU.mult).then_inc(proj_free[half], 1)

                for i in range(2):
                    for b in range(4):
                        maximum(4 * i + b)
                        if last_head:
                            add_tile(4 * i + b)
                        if b == 2:
                            silu_half(i, 0)
                        if not last_head:
                            some((2, 2, 2, 0)[b])
                    dve.wait_ge(exp_done, 8 * PAIRS + 8 * h + 4 * i + 4)
                    blocks = slice(4 * i, 4 * i + 4)
                    steps.tick(v.reciprocal(row_sum[:, blocks, 0:1], row_sum[:, blocks, 0:1]))
                    steps.wait()
                    v.tensor_scalar(inv_sum[:, blocks, 0:1], row_sum[:, blocks, 0:1], 0.5, None, ALU.mult).then_inc(inv_ready, 1)
                    silu_half(i, 1)
                for i in range(2):
                    for c in (2 * i, 2 * i + 1):
                        dve.wait_ge(t_hi, t_use + c + 1)
                        rest(ptm_lo[:, c % 2, :], ps_t[:, 1 - c % 2, :], ptm_hi[:, c % 2, :]).then_inc(t_evac, 1)
                        some(3)
                        dve.wait_ge(values_done, 2 + PT_M + 4 * h + c + 1)
                        o = sz_m[:, :, 2 * c * P:(2 * c + 2) * P]
                        v.tensor_tensor(o, ps_o[:, c % 2, :].rearrange("p (i q) -> p i q", i=2), o, ALU.mult).then_inc(o_free, 1)
                        if last_head:
                            center(2 * c)
                            center(2 * c + 1)
                            if c > 0:
                                add_square(2 * c - 2)
                                add_square(2 * c - 1)
                    if not last_head:
                        for half in range(2):
                            qm_lo_part(i, half, 2 * PAIRS + 4 * h + 4 + 2 * i + half)
                if not last_head:
                    mem_kv(w + 4, h + 1, t_use + 4, lambda: some(2))
                some(99)

            mean = ps_s[:, :, :].rearrange("p h s -> p (h s)")

            def add_tile(t):
                if t == 0:
                    dve.wait_ge(tile_done, W_MLAST)
                if t > 0:
                    steps.wait()
                    first = conv[:, 0, PAD:] if t == 1 else ln_sum[:, :]
                    last = v.tensor_tensor(ln_sum[:, :], first, conv[:, t, PAD:], ALU.add)
                    if t < KD - 1:
                        steps.tick(last)
                    else:
                        last.then_inc(lnsum_ready, 1)

            def center(t):
                if t == 0:
                    dve.wait_ge(s_ready, S_LN + 2)
                y = conv[:, t, PAD:]
                v.tensor_tensor(y, y, mean, ALU.subtract).then_inc(centered, 1)

            def add_square(t):
                dve.wait_ge(sq_ready, t + 1)
                if t == 0:
                    v.tensor_copy(ln_sum[:, :], ln_sq[:, 0, :]).then_inc(squared, 1)
                else:
                    dve.wait_ge(squared, t)
                    last = v.tensor_tensor(ln_sum[:, :], ln_sum[:, :], ln_sq[:, t % 2, :], ALU.add)
                    last.then_inc(squared if t < KD - 1 else lnsum_ready, 1)

            todo = [(4, k) for k in range(21, TAPS)] + [(c, 0) for c in (5, 6, 7)]

            def some_taps():
                for c, k in todo[:3]:
                    tap(c, k, k == 0)
                del todo[:3]

            for half in range(2):
                qm_lo_part(1, half, 2 * PAIRS + 2 + half)
            mem_kv(W_M0 + 2, 0, T_MV0, some_taps)
            while todo:
                some_taps()
            for h in steps.loop(MEM_HEADS - 1, HEAD_STEPS + 30):
                mem_head(h, W_MLOOP + 8 * h, T_MLOOP + 5 * h, False,
                         [(c, 1 + 10 * h + i) for i in range(10) for c in (5, 6, 7)])
            steps.wait()
            for c in (6, 7):
                steps.tick(v.tensor_copy(conv[:, c, PAD:], late_tiles[:, c - 6, :]))
            mem_head(MEM_HEADS - 1, W_MLAST, T_MLOOP + 5 * (MEM_HEADS - 1), True, [])

            for t in (KD - 2, KD - 1):
                add_square(t)
            ms = sums[:, MS:MS + NBLK]
            dve.wait_ge(s_ready, S_LN + 3)
            v.tensor_scalar(ms, ps_t[:, 0, 0:NBLK], LN_EPS, None, ALU.add).then_inc(var_ready, 1)
            dve.wait_ge(ln_root, 1)
            steps.tick(v.reciprocal(ms, ms))
            steps.wait()
            for b in range(NBLK):
                last = v.tensor_scalar(rstd_diag[:, b, :], ident[:, :], ms[:, b:b + 1], float(D), ALU.mult, ALU.mult)
            last.then_inc(diag_ready, 1)
            dve.wait_ge(s_ready, S_LN + 5)
            rstd = ps_s[:, :, :].rearrange("p h s -> p (h s)")

            def normalised(t):
                y = conv[:, t, PAD:]
                v.tensor_tensor(y, y, rstd, ALU.mult).then_inc(norm_ready, 1)

            def gated_c(t):
                y = conv[:, t, PAD:]
                dve.wait_ge(c_silu, t + 1)
                for half in range(2):
                    dve.wait_ge(proj_free[half], U_ZC + t + 1)
                v.tensor_tensor(y, y, sz_c[:, t % ZC_SLOTS, :], ALU.mult).then_inc(c_tile, 1)

            def c_lo(t):
                dve.wait_ge(oT_hi_done, t + 1)
                v.tensor_tensor(oT_lo[:, t, :], conv[:, t, PAD:], f32(oT_hi[:, t, :]), ALU.subtract).then_inc(oT_ready, 1)

            for t in range(4):
                normalised(t)
                if t >= 1:
                    gated_c(t - 1)
                if t >= 2:
                    c_lo(t - 2)
            gated_c(3)
            c_lo(2)
            normalised(4)
            c_lo(3)
            for t in range(4, KD):
                if t + 1 < KD:
                    normalised(t + 1)
                gated_c(t)
                c_lo(t)

            def merge_half(n, e, half):
                w, full = W_MERGE + 16 * n + 2 * e + 1, F_MERGE + 16 * n + 2 * e + 1
                wait_half(half, w, full)
                dve.wait_ge(gate_done[half], 8 * n + e + 1)
                y = flat(yT[:, ds(e, 1), half_cols(half)])
                if n == 0:
                    v.tensor_tensor(y, ps_proj[:, half, :], gate[:, half_cols(half)], ALU.mult).then_inc(proj_free[half], 1)
                else:
                    v.tensor_tensor(gate[:, half_cols(half)], ps_proj[:, half, :], gate[:, half_cols(half)],
                                    ALU.mult).then_inc(proj_free[half], 1)
                    dve.wait_ge(proj_free[half], U_MERGE + 8 * n + e + 1)
                    last = v.tensor_tensor(y, y, gate[:, half_cols(half)], ALU.add)
                    last.then_inc(merged, 1)

            for n in range(3):
                if n > 0:
                    for k in range(KD):
                        i = KD * (n - 1) + k
                        dve.wait_ge(oT_hi_done, KD * n + k + 1)
                        v.tensor_tensor(oT_lo[:, k, :], o_raw[:, i % RAW_SLOTS, :], f32(oT_hi[:, k, :]),
                                        ALU.subtract).then_inc(oT_ready, 1)
                with dve.Fori(0, KD) as e:
                    for half in range(2):
                        merge_half(n, e, half)

            for k in range(KD):
                dve.wait_ge(y_hi, k + 1)
                v.tensor_tensor(oT_lo[:, k, :], yT[:, k, :], f32(oT_hi[:, k, :]), ALU.subtract).then_inc(y_ready, 1)
            dve.wait_ge(oT_ready, 3 * KD)
            banks_of = [ps_s, ps_t, ps_o, ps_proj]

            def residual(s):
                dve.wait_ge(out_ready, s + 1)
                dve.wait_ge(x2_in[s % 2], 16 * (s // 2 + 1))
                if s >= 2:
                    dve.wait_ge(stored[s % 2], 16 * (s // 2))
                v.tensor_tensor(o_raw[:, s % 2, :], banks_of[s % 4][:, :, :].rearrange("p h s -> p (h s)"),
                                raw[:, s % 2, :], ALU.add).then_inc(resid, 1)

            def finish(s):
                dve.wait_ge(out_ss, s + 1)
                v.tensor_scalar(sums[:, MS + s:MS + s + 1], sums[:, s:s + 1], 1.0 / D, RMS_EPS, ALU.mult, ALU.add).then_inc(out_ms, 1)
                dve.wait_ge(out_root, s + 1)
                steps.tick(v.reciprocal(sums[:, MS + s:MS + s + 1], sums[:, MS + s:MS + s + 1]))
                steps.wait()
                dve.wait_ge(fg_in, 16)
                v.scalar_tensor_tensor(out=o_raw[:, s % 2, :], in0=o_raw[:, s % 2, :], scalar=sums[:, MS + s:MS + s + 1],
                                       in1=gate, op0=ALU.mult, op1=ALU.mult).then_inc(out_row, 1)

            for s in range(NBLK):
                residual(s)
                finish(s)


def bucket_of_distance(n):
    import math
    exact = BUCKETS // 2
    if n < exact:
        return n
    return min(exact + int(math.log(n / exact) / math.log(WINDOW / exact) * (BUCKETS - exact)), BUCKETS - 1)


_INS = ["x", "mem", "rel_bias", "norm_g", "w_in", "sinks", "conv_w", "conv_b", "conv_ln_g", "conv_ln_b",
        "mem_norm_g", "w_mem_kv", "w_branch", "w_out", "final_norm_g"]


def kernel(**inputs):
    import numpy as np
    import concourse.bacc as bacc
    from concourse.bass_utils import run_bass_kernel_spmd

    nc = bacc.Bacc("TRN2", target_bir_lowering=False, num_devices=1)
    arrays, args = {}, []
    onehot = np.zeros((BUCKETS, WINDOW), np.float32)
    for u in range(WINDOW):
        onehot[bucket_of_distance(WINDOW - 1 - u), u] = 1.0
    for name in _INS + ["bucket_onehot"]:
        a = onehot if name == "bucket_onehot" else np.ascontiguousarray(inputs[name])
        arrays[f"in_{name}"] = a
        args.append(nc.dram_tensor(f"in_{name}", a.shape, mybir.dt.from_np(a.dtype), kind="ExternalInput").ap())
    out = nc.dram_tensor("out", (1, S, D), F32, kind="ExternalOutput").ap()
    build(nc, *args, out)
    r = run_bass_kernel_spmd(nc, [arrays], core_ids=[0])
    return r.results[0]["out"]
```
